# Optimizing a Trainium2 kernel written in Bass

```python
import jax, jax.numpy as jnp
from jax import lax
import numpy as np

D_MODEL = 1024
BATCH = 1
SEQ = 1024
DEPTH = 1

CHUNK = 64
N_META = 16
A_HEADS = 4
A_DK = 128
A_DV = 128
A_WIDTH = A_HEADS * A_DK
B_Q_HEADS = 8
B_KV_HEADS = 2
B_HEAD_DIM = 64
B_GROUP = B_Q_HEADS // B_KV_HEADS
B_WIDTH = B_Q_HEADS * B_HEAD_DIM
B_KV_WIDTH = B_KV_HEADS * B_HEAD_DIM
WINDOW = 128
WINDOW_CHUNKS = WINDOW // CHUNK
ROPE_THETA = 500000.0
ROPE_DIM = B_HEAD_DIM // 4
D_FF = 4 * D_MODEL
LN_EPS = 1e-5
RMS_EPS = 1e-6
ALPHA = (2 * DEPTH) ** 0.25
BETA = (8 * DEPTH) ** -0.25
NEG = -1e30

IN_SEGMENTS = (
    (A_WIDTH, 1.0),
    (A_WIDTH, 1.0),
    (A_HEADS * A_DV, BETA),
    (A_HEADS * A_DV, 1.0),
    (B_WIDTH, 1.0),
    (B_KV_WIDTH, 1.0),
    (B_KV_WIDTH, BETA),
    (D_MODEL, 1.0),
    (D_MODEL, 1.0),
)
IN_COLS = sum(s for s, _ in IN_SEGMENTS)

kernel_name = "hybrid_hgrn2_swa_sink_block"

def layer_norm(x, g, b):
    xf = x.astype(jnp.float32)
    mu = jnp.mean(xf, -1, keepdims=True)
    var = jnp.mean(jnp.square(xf - mu), -1, keepdims=True)
    y = (xf - mu) * lax.rsqrt(var + LN_EPS) * g.astype(jnp.float32) + b.astype(jnp.float32)
    return y.astype(x.dtype)

def partial_rope(x, pos):
    half = ROPE_DIM // 2
    inv = jnp.power(jnp.float32(ROPE_THETA), -jnp.arange(half, dtype=jnp.float32) / half)
    ang = pos.astype(jnp.float32)[:, None] * inv[None, :]
    cos = jnp.cos(ang)[None, :, None, :]
    sin = jnp.sin(ang)[None, :, None, :]
    xr = x[..., :ROPE_DIM].astype(jnp.float32)
    x1, x2 = xr[..., :half], xr[..., half:]
    rot = jnp.concatenate([x1 * cos - x2 * sin, x2 * cos + x1 * sin], -1).astype(x.dtype)
    return jnp.concatenate([rot, x[..., ROPE_DIM:]], -1)

def sink_softmax(s, sink):
    sk = jnp.broadcast_to(sink.astype(jnp.float32)[:, :, None, None], s.shape[:-1] + (1,))
    p = jax.nn.softmax(jnp.concatenate([s, sk], -1), axis=-1)
    return p[..., :-1]

def swa_sink_attention(q, k, v, sink):
    bsz, L = q.shape[0], q.shape[1]
    n_chunks = (L - N_META) // CHUNK
    scale = B_HEAD_DIM ** -0.5
    qg = q.reshape(bsz, L, B_KV_HEADS, B_GROUP, B_HEAD_DIM)
    q_m = qg[:, :N_META]
    q_r = qg[:, N_META:].reshape(bsz, n_chunks, CHUNK, B_KV_HEADS, B_GROUP, B_HEAD_DIM)
    k_m, v_m = k[:, :N_META], v[:, :N_META]
    k_r = k[:, N_META:].reshape(bsz, n_chunks, CHUNK, B_KV_HEADS, B_HEAD_DIM)
    v_r = v[:, N_META:].reshape(bsz, n_chunks, CHUNK, B_KV_HEADS, B_HEAD_DIM)

    s_m = jnp.einsum('bqjgd,bkjd->bjgqk', q_m, k_m).astype(jnp.float32) * scale
    p_m = sink_softmax(s_m, sink)
    o_m = jnp.einsum('bjgqk,bkjd->bqjgd', p_m.astype(v.dtype), v_m)
    o_m = o_m.reshape(bsz, N_META, B_WIDTH)

    def shift(a, w):
        return jnp.concatenate([jnp.zeros_like(a[:, :w]), a[:, :-w]], 1)
    meta_k = jnp.broadcast_to(k_m[:, None], (bsz, n_chunks) + k_m.shape[1:])
    meta_v = jnp.broadcast_to(v_m[:, None], (bsz, n_chunks) + v_m.shape[1:])
    shifts = list(range(WINDOW_CHUNKS - 1, 0, -1))
    k_win = jnp.concatenate([meta_k] + [shift(k_r, w) for w in shifts] + [k_r], 2)
    v_win = jnp.concatenate([meta_v] + [shift(v_r, w) for w in shifts] + [v_r], 2)
    j = jnp.arange(n_chunks)
    valid = jnp.concatenate(
        [jnp.ones((n_chunks, N_META), bool)]
        + [jnp.broadcast_to((j >= w)[:, None], (n_chunks, CHUNK)) for w in shifts]
        + [jnp.ones((n_chunks, CHUNK), bool)], 1)
    s = jnp.einsum('bncjgd,bnkjd->bnjgck', q_r, k_win).astype(jnp.float32) * scale
    s = jnp.where(valid[None, :, None, None, None, :], s, NEG)
    p = sink_softmax(s, sink)
    o_r = jnp.einsum('bnjgck,bnkjd->bncjgd', p.astype(v.dtype), v_win)
    o_r = o_r.reshape(bsz, n_chunks * CHUNK, B_WIDTH)
    return jnp.concatenate([o_m, o_r], 1)

def hgrn2_chunk(state, q, k, v, log_f):
    c = q.shape[1]
    b = jnp.cumsum(log_f, axis=1)
    causal = jnp.tril(jnp.ones((c, c), bool))
    diff = b[:, :, None] - b[:, None, :]
    decay = jnp.exp(jnp.where(causal[None, :, :, None, None], diff, -jnp.inf))
    attn = jnp.einsum('bthk,bshk,btshk->bhts', q, k, decay)
    o = jnp.einsum('bhts,bshv->bthv', attn, v)
    o = o + jnp.einsum('bthk,bhkv->bthv', q * jnp.exp(b), state)
    b_last = b[:, -1]
    k_dec = k * jnp.exp(b_last[:, None] - b)
    new_state = jnp.exp(b_last)[..., None] * state + jnp.einsum('bshk,bshv->bhkv', k_dec, v)
    return new_state, o

def hgrn2_mix(q, k, v, log_f):
    bsz, L = q.shape[0], q.shape[1]
    n_chunks = (L - N_META) // CHUNK
    s0 = jnp.zeros((bsz, A_HEADS, A_DK, A_DV), jnp.float32)
    s_meta, o_meta = hgrn2_chunk(s0, q[:, :N_META], k[:, :N_META], v[:, :N_META], log_f[:, :N_META])

    def to_chunks(a):
        a = a[:, N_META:].reshape(bsz, n_chunks, CHUNK, a.shape[2], a.shape[3])
        return jnp.swapaxes(a, 0, 1)

    def step(s, inp):
        return hgrn2_chunk(s, *inp)

    _, o_r = lax.scan(step, s_meta, (to_chunks(q), to_chunks(k), to_chunks(v), to_chunks(log_f)))
    o_r = jnp.swapaxes(o_r, 0, 1).reshape(bsz, n_chunks * CHUNK, A_HEADS, A_DV)
    return jnp.concatenate([o_meta, o_r], 1)

def hgrn2_branch(q_pre, f_pre, i_in, g_pre, lower_bound, norm_g):
    bsz, L = q_pre.shape[0], q_pre.shape[1]
    q = jax.nn.silu(q_pre.astype(jnp.float32)).reshape(bsz, L, A_HEADS, A_DK)
    lb = lower_bound.reshape(A_HEADS, A_DK)
    f = lb + (1.0 - lb) * jax.nn.sigmoid(f_pre.astype(jnp.float32).reshape(bsz, L, A_HEADS, A_DK))
    k = 1.0 - f
    v = i_in.astype(jnp.float32).reshape(bsz, L, A_HEADS, A_DV)
    o = hgrn2_mix(q, k, v, jnp.log(f))
    o = o * lax.rsqrt(jnp.mean(jnp.square(o), -1, keepdims=True) + RMS_EPS)
    o = o.reshape(bsz, L, A_HEADS * A_DV) * norm_g.astype(jnp.float32)
    o = o * jax.nn.silu(g_pre.astype(jnp.float32))
    return o.astype(q_pre.dtype)

def setup_inputs(seed: int = 0) -> dict:
    key = jax.random.key(seed)
    ks = jax.random.split(key, 20)

    def nrm(k, shape, s):
        return jax.random.normal(k, shape, jnp.float32) * s

    col_scale = jnp.concatenate([jnp.full((n,), s, jnp.float32) for n, s in IN_SEGMENTS])
    return {
        "x": nrm(ks[0], (BATCH, SEQ, D_MODEL), 1.0),
        "meta_tokens": nrm(ks[1], (N_META, D_MODEL), 1.0),
        "ln_emb_g": 1.0 + nrm(ks[2], (D_MODEL,), 0.02),
        "ln_emb_b": nrm(ks[3], (D_MODEL,), 0.02),
        "w_in": nrm(ks[4], (DEPTH, D_MODEL, IN_COLS), D_MODEL ** -0.5) * col_scale,
        "b_gate": nrm(ks[5], (DEPTH, 2 * D_MODEL), 0.02),
        "lb_logits": nrm(ks[6], (DEPTH + 1, A_WIDTH), 0.5),
        "a_norm_g": 1.0 + nrm(ks[7], (DEPTH, A_HEADS * A_DV), 0.02),
        "sink": nrm(ks[8], (DEPTH, B_Q_HEADS), 0.5),
        "w_proj_a": nrm(ks[9], (DEPTH, A_HEADS * A_DV, D_MODEL), (A_HEADS * A_DV) ** -0.5),
        "w_proj_b": nrm(ks[10], (DEPTH, B_WIDTH, D_MODEL), B_WIDTH ** -0.5),
        "w_o": nrm(ks[11], (DEPTH, D_MODEL, D_MODEL), D_MODEL ** -0.5 * BETA),
        "ln1_g": 1.0 + nrm(ks[12], (DEPTH, D_MODEL), 0.02),
        "ln1_b": nrm(ks[13], (DEPTH, D_MODEL), 0.02),
        "w_up": nrm(ks[14], (DEPTH, D_MODEL, D_FF), D_MODEL ** -0.5),
        "w_down": nrm(ks[15], (DEPTH, D_FF, D_MODEL), D_FF ** -0.5 * BETA),
        "ln2_g": 1.0 + nrm(ks[16], (DEPTH, D_MODEL), 0.02),
        "ln2_b": nrm(ks[17], (DEPTH, D_MODEL), 0.02),
    }

def reference(x, meta_tokens, ln_emb_g, ln_emb_b, w_in, b_gate, lb_logits, a_norm_g, sink,
              w_proj_a, w_proj_b, w_o, ln1_g, ln1_b, w_up, w_down, ln2_g, ln2_b):
    bsz = x.shape[0]
    meta = jnp.broadcast_to(meta_tokens.astype(x.dtype)[None], (bsz, N_META, D_MODEL))
    h = layer_norm(jnp.concatenate([meta, x], 1), ln_emb_g, ln_emb_b)
    L = h.shape[1]
    pos = jnp.arange(L, dtype=jnp.int32)
    lower_bounds = jnp.cumsum(jax.nn.softmax(lb_logits.astype(jnp.float32), axis=0), axis=0)
    split_idx = [int(v) for v in np.cumsum([n for n, _ in IN_SEGMENTS])[:-1]]

    for l in range(DEPTH):
        proj = h @ w_in[l]
        a_q, a_f, a_i, a_g, b_q, b_k, b_v, g_a, g_b = jnp.split(proj, split_idx, axis=-1)
        out_a = hgrn2_branch(a_q, a_f, a_i, a_g, lower_bounds[l], a_norm_g[l])
        q = partial_rope(b_q.reshape(bsz, L, B_Q_HEADS, B_HEAD_DIM), pos)
        k = partial_rope(b_k.reshape(bsz, L, B_KV_HEADS, B_HEAD_DIM), pos)
        v = b_v.reshape(bsz, L, B_KV_HEADS, B_HEAD_DIM)
        out_b = swa_sink_attention(q, k, v, sink[l].reshape(B_KV_HEADS, B_GROUP))
        gates = jax.nn.sigmoid((jnp.concatenate([g_a, g_b], -1) + b_gate[l]).astype(jnp.float32)).astype(h.dtype)
        merged = gates[..., :D_MODEL] * (out_a @ w_proj_a[l]) + gates[..., D_MODEL:] * (out_b @ w_proj_b[l])
        h = layer_norm(ALPHA * h + merged @ w_o[l], ln1_g[l], ln1_b[l])
        ff = jnp.square(jax.nn.relu(h @ w_up[l])) @ w_down[l]
        h = layer_norm(ALPHA * h + ff, ln2_g[l], ln2_b[l])

    return h[:, N_META:]


_drawn_inputs = setup_inputs


def setup_inputs(seed=0):
    import zlib

    import numpy as np

    out = dict(_drawn_inputs(seed))
    spreads = {}
    factors = {'meta_tokens': 5.953,
     'b_gate': 8.0,
     'lb_logits': 5.724,
     'a_norm_g': 25.968,
     'sink': 200.0,
     'ln1_g': 2.776,
     'ln2_g': 23.454,
     'ln2_b': 23.53,
     'w_proj_b': 11.345,
     'ln1_b': 6.706}
    for name, (base, spread) in spreads.items():
        noise = np.random.default_rng([zlib.crc32(name.encode()), seed]).standard_normal(out[name].shape)
        drawn = base * np.exp(spread * noise) if base else spread * noise
        out[name] = __import__('jax').numpy.asarray(drawn.astype(out[name].dtype))
    for name, factor in factors.items():
        out[name] = (out[name] * factor).astype(out[name].dtype)
    return out
```

```python
import numpy as np
import concourse.bass as bass
from concourse import mybir

P = 128
D = 1024
T = 1024
META = 16
CHUNK = 64
TA = T + META
NT = T // P
KT = D // P
HEADS = 4
QH = 8
FF = 4096
NBLK = 8
FT = FF // NBLK // P
HALF = 512
LN_EPS = 1e-5
RMS_EPS = 1e-6
ALPHA = 2.0 ** 0.25
SCALE = 64 ** -0.5
TINY = 1e-19
NEG = -1e30
LEVELS = [32, 16, 8, 4, 2, 1]
NL = len(LEVELS)
KD, QE = NL, NL + 1
SLOTS = 8
C_Q, C_F, C_I, C_G, C_BQ, C_BK, C_GATE = 0, 512, 1024, 1536, 2048, 2560, 2816

F32 = mybir.dt.float32
F32R = mybir.dt.float32r
ALU = mybir.AluOpType
ACT = mybir.ActivationFunctionType
AX = mybir.AxisListType.X

N_C = 22
N_D = N_C + 2 * NT
N_E = N_D + 8
N_F = N_E + 8
SLOT_GA, SLOT_GB = 6, 7


class Tally:

    def __init__(self, sem):
        self.sem, self.n, self.var, self.per = sem, 0, None, 0

    def now(self):
        return self.n if self.var is None else self.n + self.var * self.per

    def begin(self, var, per):
        self.var, self.per, self.start = var, per, self.n

    def end(self, times):
        assert self.n - self.start == self.per, (self.n - self.start, self.per)
        self.n = self.start + self.per * times
        self.var = None


def build(nc, x, meta_tokens, ln_emb_g, ln_emb_b, w_in, b_gate, lb_logits, a_norm_g, sink, w_proj_a,
          w_proj_b, w_o, ln1_g, ln1_b, w_up, w_down, ln2_g, ln2_b, c_ident, c_mask, c_rope, out):
    x = x.rearrange("b t d -> (b t) d")
    out = out.rearrange("b t d -> (b t) d")
    w_in = w_in.rearrange("l k n -> (l k) n")
    w_pa = w_proj_a.rearrange("l k n -> (l k) n")
    w_pb = w_proj_b.rearrange("l k n -> (l k) n")
    w_o = w_o.rearrange("l k n -> (l k) n")
    w_up = w_up.rearrange("l k n -> (l k) n")
    w_down = w_down.rearrange("l k n -> (l k) n")

    def internal(name, shape):
        return nc.dram_tensor(name, shape, F32, kind="Internal").ap()

    pair_d = internal("pair_scratch", [NT, P, 6, HALF])
    kT_d = internal("kT_scratch", [P, 2, CHUNK + T])
    vb_d = internal("vb_scratch", [CHUNK + T, P])
    gate_d = internal("gate_scratch", [2, KT, P, T])
    mix_d = internal("mix_scratch", [2, NT, P, HALF])
    h_d = internal("h_scratch", [NT, P, D])
    h1_d = internal("h1_scratch", [NT, P, D])

    base = [16512]
    limit = 229344

    def sb(name, shape, dt=F32, at=None):
        o = base[0] if at is None else at
        nbytes = 4 * int(np.prod(shape[1:]))
        t = nc.alloc_sbuf_tensor_at(name, shape, dt, offset=o)
        if at is None:
            base[0] = (o + nbytes + 31) // 32 * 32
        assert o + nbytes <= limit, (name, o + nbytes)
        return t

    R1 = base[0]
    hT_hi = sb("hT_hi", [P, KT, TA], F32R)
    hT_lo = sb("hT_lo", [P, KT, TA], F32R)
    mT_hi = sb("mT_hi", [P, KT, T], F32R, at=R1)
    mT_lo = sb("mT_lo", [P, KT, T], F32R, at=R1 + 4 * KT * T)
    u_hi = sb("u_hi", [P, FT, T], F32R, at=R1)
    u_lo = sb("u_lo", [P, FT, T], F32R, at=R1 + 4 * FT * T)
    y = sb("y", [P, NT, D], F32, at=R1 + 8 * FT * T)
    w_hi = sb("w_hi", [P, SLOTS, D], F32R)
    RL = base[0]
    w_lo = sb("w_lo", [P, SLOTS, D], F32R)
    w_raw = sb("w_raw", [P, SLOTS, D], F32, at=RL)
    ident = sb("ident", [P, P])
    lbl = sb("lbl", [P, 2, HEADS])
    lbe = sb("lbe", [P, 2, HEADS])
    lbm = sb("lbm", [P, HEADS])
    lb = sb("lb", [P, HEADS])
    oml = sb("oml", [P, HEADS])
    noml = sb("noml", [P, HEADS])
    normg = sb("normg", [P, HEADS])
    bgate = sb("bgate", [P, 2, KT])
    sinks = sb("sinks", [P, QH])
    negsink = sb("negsink", [P, QH])
    stats = sb("stats", [P, 2, 2, 6])
    mv = sb("mv", [P, 2, 2])
    rstd = sb("rstd", [P, 2, 2])
    neghalf = sb("neghalf", [P, 4])
    yscale = sb("yscale", [P, NBLK])
    R2 = base[0] = (base[0] + 31) // 32 * 32
    xb = sb("xb", [P, 3, D])
    lng = sb("lng", [P, D])
    lnb = sb("lnb", [P, D])
    fst = sb("fst", [P, HEADS, TA])
    st = sb("st", [P, 6, HALF])
    sg = sb("sg", [P, 2, HALF])
    qtm = sb("qtm", [P, 2, HALF])
    A_end = base[0]
    ktm = sb("ktm", [P, 2, 2, 2, 64], at=R2)
    kTs = sb("kTs", [P, 2, 2, P], at=R2 + 2048)
    vst = sb("vst", [P, 2, P], at=R2 + 4096)
    rope = sb("rope", [P, NT + 1, 2, 8], at=R2 + 5120)
    rtmp = sb("rtmp", [P, 4, QH * 8], at=R2 + 5120 + 576)
    scanmask = sb("scanmask", [P, TA], at=R2 + 12288)
    kmeta = sb("kmeta", [P, HEADS, META], at=R2 + 12288 + 4160)
    dmeta = sb("dmeta", [P, HEADS, META], at=R2 + 12288 + 4416)
    vmeta = sb("vmeta", [META, HALF])
    kTm = sb("kTm", [P, 2, META])
    vmb = sb("vmb", [P, HALF])
    zero = sb("zero", [P, P])
    negm = sb("negm", [P, P])
    ones = sb("ones", [P, CHUNK])
    pin = sb("pin", [P, 3, HALF])
    S0 = sb("S0", [P, HEADS, P])
    kwin = sb("kwin", [P, 2, 3 * CHUNK])
    vwin = sb("vwin", [P, 2, P])
    C_keep = base[0]
    base[0] = R2
    X = sb("X", [P, NL + 2, HALF])
    masks = sb("masks", [P, HALF])
    Amat = sb("Amat", [P, HEADS, P])
    prod = sb("prod", [P, HEADS, 384])
    pv_ = sb("pv", [P, HALF])
    pg = sb("pg", [P, HALF])
    pqT = sb("pqT", [P, HEADS, P])
    prob = sb("prob", [P, QH, META + P])
    probT = sb("probT", [P, QH, P])
    probm = sb("probm", [P, P])
    probmT = sb("probmT", [P, P])
    kdT = sb("kdT", [P, HALF])
    S1 = sb("S1", [P, HEADS, P])
    o_sb = sb("o_sb", [P, HEADS, P])
    osq = sb("osq", [P, HEADS, P])
    ob = sb("ob", [P, QH, 64])
    gst = sb("gst", [P, 2, HALF])
    assert base[0] <= A_end, (base[0], A_end)
    base[0] = C_keep
    oast = sb("oast", [P, HALF])
    obst = sb("obst", [P, HALF])
    decay = sb("decay", [P, HEADS, 2])
    rowmax = sb("rowmax", [P, QH])
    negmax = sb("negmax", [P, QH])
    sinkexp = sb("sinkexp", [P, QH])
    rowsum = sb("rowsum", [P, QH])
    rden = sb("rden", [P, QH])
    osum = sb("osum", [P, HEADS])
    orms = sb("orms", [P, HEADS])
    base[0] = R2
    mix_hi = sb("mix_hi", [P, 2, NT, HALF], F32R)
    RX = base[0]
    mix_lo = sb("mix_lo", [P, 2, NT, HALF], F32R)
    mix_raw = sb("mix_raw", [P, 2, NT, HALF], F32, at=RX)
    RE = base[0]
    gt = sb("gt", [P, 2, 2, HALF])
    t1 = sb("t1", [P, HALF])
    t2 = sb("t2", [P, HALF])
    h1T_hi = sb("h1T_hi", [P, KT, T], F32R, at=R2)
    h1T_lo = sb("h1T_lo", [P, KT, T], F32R, at=RX)
    base[0] = RE
    hb = sb("hb", [P, D])
    l1g = sb("l1g", [P, D])
    l1b = sb("l1b", [P, D])
    base[0] = RE
    ur = sb("ur", [P, 2, HALF])
    us = sb("us", [P, 2, HALF])
    l2g = sb("l2g", [P, D], at=RE)
    l2b = sb("l2b", [P, D], at=RE + 4096)
    assert mix_hi is not None

    ps_guard = nc.psum_tensor("ps", [P, 8, HALF], F32)
    ps = ps_guard.__enter__()

    names = {}

    def sem(name):
        names[name] = nc.semaphore(name)
        return names[name].__enter__()

    x_in = [sem(f"x_in{i}") for i in range(3)]
    tab_in = sem("tables_in")
    small_in = sem("small_tables_in")
    rope_in = sem("rope_in")
    h_saved = [sem(f"h_saved{i}") for i in range(3)]
    st_saved = [sem(f"stage_saved{i}") for i in range(6)]
    kv_saved = [sem(f"kv_saved{i}") for i in range(2)]
    pad_saved = sem("pads_saved")
    b_saved = sem("b_saved")
    vmb_in = sem("vmeta_blocks_in")
    w_landed = [sem(f"w_landed{i}") for i in range(SLOTS)]
    qkb_in, v_in, g_in, q_in, vw_in = sem("qkb_in"), sem("v_in"), sem("g_in"), sem("qT_in"), sem("vwin_in")
    mask_in = sem("masks_in")
    gate_saved = [sem(f"gate_saved{i}") for i in range(2)]
    oa_saved, ob_saved = sem("oa_saved"), sem("ob_saved")
    mix_in = [sem(f"mix_in{i}") for i in range(4)]
    gt_in = [sem(f"gt_in{i}") for i in range(2)]
    hb_in, h1_saved, l1_in, y_in, l2_in, out_saved = (sem("hb_in"), sem("h1_saved"), sem("ln1_in"), sem("y_in"),
                                                      sem("ln2_in"), sem("out_saved"))
    w_split = sem("w_split")
    pool_const, pool_rstd, pool_D, pool_probm, pool_orms = (sem("pool_const"), sem("pool_rstd"), sem("pool_D"),
                                                            sem("pool_probm"), sem("pool_orms"))
    pool_seq = sem("pool_seq")
    pool_passed, act_passed = sem("pool_passed"), sem("act_passed")
    pe_hT, pe_tm, pe_cm, pe_fm, pe_qT, pe_kT, pe_meta = (sem("pe_hT"), sem("pe_tm"), sem("pe_cm"), sem("pe_fmeta"),
                                                         sem("pe_qT"), sem("pe_kT"), sem("pe_meta"))
    pe_lv, pe_kdT, pe_gate, pe_U, pe_sc, pe_o, pe_PT, pe_PV, pe_oT, pe_obT = (
        sem(n) for n in ("pe_levels", "pe_kdT", "pe_gate", "pe_U", "pe_scores", "pe_o", "pe_probT", "pe_PV", "pe_oT",
                         "pe_obT"))
    pe_mix, pe_wo, pe_h1T, pe_up, pe_down = (sem("pe_mix"), sem("pe_wo"), sem("pe_h1T"), sem("pe_up"), sem("pe_down"))
    act_lb, act_hi, act_tm, act_cm, act_fm, act_qT, act_kT, act_ln, act_meta = (
        sem(n) for n in ("act_lb", "act_hT_hi", "act_tm", "act_cm", "act_fmeta", "act_qT", "act_kT", "act_ln",
                         "act_meta"))
    act_kdT, act_gate, act_prob, act_es, act_E, act_E7, act_dec, act_o, act_PT, act_ob = (
        sem(n) for n in ("act_kdT", "act_gate", "act_prob", "act_sinkexp", "act_E", "act_E_qe", "act_decay", "act_o",
                         "act_probT", "act_ob"))
    act_mixhi, act_sig, act_mhi, act_h1hi, act_ur, act_uhi = (sem(n) for n in (
        "act_mix_hi", "act_sig", "act_m_hi", "act_h1T_hi", "act_relu", "act_u_hi"))
    dve_seq = sem("dve_seq")
    dve_const, dve_lb, dve_stats, dve_h, dve_lo, dve_rope, dve_krope, dve_k, dve_f, dve_scan, dve_meta, dve_kdm, \
        dve_silu = (sem(n) for n in ("dve_const", "dve_lb", "dve_stats", "dve_h", "dve_hT_lo", "dve_rope",
                                     "dve_krope", "dve_k", "dve_f", "dve_scan", "dve_metasub", "dve_kdmeta",
                                     "dve_silu"))
    dve_prod, dve_A, dve_S, dve_nb, dve_osum, dve_X, dve_Xq, dve_on, dve_oa, dve_ob, dve_snk = (
        sem(n) for n in ("dve_prod", "dve_A", "dve_S", "dve_negmax", "dve_osum", "dve_X", "dve_X_qe", "dve_on",
                         "dve_oa", "dve_ob", "dve_sink"))
    dve_mixlo, dve_m, dve_mlo, dve_r, dve_h1, dve_h1lo, dve_us, dve_ulo, dve_y, dve_out = (
        sem(n) for n in ("dve_mix_lo", "dve_m", "dve_m_lo", "dve_r", "dve_h1", "dve_h1T_lo", "dve_usq",
                         "dve_u_lo", "dve_y", "dve_out"))

    def seen(eng, s, v):
        if not (isinstance(v, int) and v <= 0):
            eng.wait_ge(s, v)

    def passed(eng, s, v):
        if not isinstance(v, int):
            eng.sem_inc(s, 1)

    def kview(w, cols, k0=0, kn=KT):
        return w[k0 * P:(k0 + kn) * P, cols].rearrange("(k p) n -> p k n", p=P)

    def slot(t, s, k):
        return t[:, s, :].rearrange("p (k n) -> p k n", k=k)

    def as_pairs(t):
        return t.rearrange("p (q n) -> p q n", n=P)

    block_guard = nc.Block()
    block = block_guard.__enter__()

    def cols(c, n):
        return slice(c, c + n)

    a_granules = [kview(w_in, cols(C_I, HALF), 2 * g, 2) for g in range(4)]
    a_granules += [kview(w_in, cols(C_BQ, HALF), 2 * g, 2) for g in range(4)]
    a_granules += [kview(w_in, cols(C_BK, 256), 4 * g, 4) for g in range(2)]
    for c in (C_F, C_Q, C_G):
        a_granules += [kview(w_in, cols(c + P * j, P)) for j in range(4)]
    assert len(a_granules) == N_C

    def a_slot_free(n):
        m = n - SLOTS
        if m < 4:
            return pe_tm, 9
        if m < 8:
            return pe_tm, 17
        if m < 10:
            return pe_tm, 26
        return pe_fm, m - 9

    def st_free(eng, idx):
        seen(eng, st_saved[idx % 6], 16 * (idx // 6))

    def st_all_saved(eng, before):
        for i in range(6):
            eng.wait_ge(st_saved[i], 16 * len(range(i, before, 6)))

    @block.sync
    def _(sp):
        def load_weights(src, s, k):
            return nc.sync.dma_start(slot(w_raw, s, k), src)

        def x_tile(t):
            if t >= 3:
                sp.wait_ge(pe_hT, t - 2)
                sp.wait_ge(h_saved[t % 3], 16 * (t // 3))
            if t < NT:
                sp.dma_start(xb[:, t % 3, :], x[P * t:P * (t + 1), :]).then_inc(x_in[t % 3], 16)
            else:
                sp.dma_start(xb[0:META, t % 3, :], meta_tokens).then_inc(x_in[t % 3], 16)

        x_tile(0)
        sp.dma_start(lng[:, :], ln_emb_g.partition_broadcast(P)).then_inc(tab_in, 16)
        sp.dma_start(lnb[:, :], ln_emb_b.partition_broadcast(P)).then_inc(tab_in, 16)
        sp.dma_start(ident[:, :], c_ident).then_inc(tab_in, 16)
        for n in range(4):
            load_weights(a_granules[n], n, 2).then_inc(w_landed[n], 16)
        x_tile(1)
        x_tile(2)
        with nc.allow_non_contiguous_dma(reason="small per-channel tables"):
            sp.dma_start(lbl[:, :, :], lb_logits.rearrange("a (h p) -> p a h", p=P)).then_inc(small_in, 16)
            sp.dma_start(normg[:, :], a_norm_g.rearrange("l (h p) -> p (l h)", p=P)).then_inc(small_in, 16)
            sp.dma_start(bgate[:, :, :], b_gate.rearrange("l (a k p) -> p (l a) k", a=2, p=P)).then_inc(small_in, 16)
        sp.dma_start(sinks[:, :], sink[0].partition_broadcast(P)).then_inc(small_in, 16)
        for n in range(4, SLOTS):
            load_weights(a_granules[n], n, 2).then_inc(w_landed[n], 16)
        sp.wait_ge(pool_const, 1)
        sp.dma_start(kT_d[:, :, 0:CHUNK], zero[:, :].rearrange("p (j n) -> p j n", j=2)).then_inc(pad_saved, 16)
        sp.dma_start(vb_d[0:CHUNK, :], zero[0:CHUNK, :]).then_inc(pad_saved, 16)
        for t in range(3, NT + 1):
            x_tile(t)
        sp.wait_ge(pe_hT, NT + 1)
        for i in range(3):
            sp.wait_ge(h_saved[i], (48, 48, 32)[i])
        sp.dma_start(rope[:, :, :, :], c_rope).then_inc(rope_in, 16)
        for n in range(SLOTS, N_C):
            sp.wait_ge(*a_slot_free(n))
            k = 2 if n < 8 else (4 if n < 10 else 8)
            load_weights(a_granules[n], n % SLOTS, k).then_inc(w_landed[n % SLOTS], 16)
            if n == 10:
                sp.wait_ge(act_tm, 26)
                sp.wait_ge(dve_const, 1)
                for h in range(QH):
                    j = h // 4
                    sp.dma_start(vmb[META * h:META * (h + 1), 64 * h:64 * (h + 1)],
                                 vst[0:META, 0, 64 * j:64 * (j + 1)]).then_inc(vmb_in, 16)

        def load_qkb(p):
            sp.dma_start(pin[:, :, :], pair_d[bass.ds(p, 1), :, 0:3, :].rearrange("a p s n -> p (a s) n")
                         ).then_inc(qkb_in, 16)

        def load_att(p):
            sp.dma_start(pqT[:, :, :].rearrange("p h n -> p (h n)"),
                         pair_d[bass.ds(p, 1), :, 5, :].rearrange("a p n -> p (a n)")).then_inc(q_in, 16)
            sp.dma_start(kwin[:, :, :], kT_d[:, :, bass.ds(P * p, 3 * CHUNK)]).then_inc(q_in, 16)

        def load_v(p):
            sp.dma_start(pv_[:, :], pair_d[bass.ds(p, 1), :, 3, :].rearrange("a p n -> p (a n)")).then_inc(v_in, 16)

        def load_vwin(p):
            sp.dma_start(vwin[:, 0, :], vb_d[bass.ds(P * p, P), :]).then_inc(vw_in, 16)
            sp.dma_start(vwin[:, 1, :], vb_d[bass.ds(P * p + CHUNK, P), :]).then_inc(vw_in, 16)

        def load_g(p):
            sp.dma_start(pg[:, :], pair_d[bass.ds(p, 1), :, 4, :].rearrange("a p n -> p (a n)")).then_inc(g_in, 16)

        def load_gate(p, which):
            s = (SLOT_GA, SLOT_GB)[which]
            load_weights(w_in[:, bass.ds(C_GATE + D * which + P * p, P)].rearrange("(k p) n -> p k n", p=P), s, 8
                         ).then_inc(w_landed[s], 16)

        sp.wait_ge(pe_cm, 10)
        load_gate(0, 0)
        sp.wait_ge(pe_cm, 12)
        load_gate(0, 1)
        sp.wait_ge(b_saved, 64)
        st_all_saved(sp, 32)
        load_qkb(0)
        for i in range(2):
            sp.wait_ge(kv_saved[i], 128)
        sp.wait_ge(pad_saved, 32)
        load_vwin(0)
        sp.wait_ge(dve_scan, 4)
        sp.wait_ge(dve_kdm, 1)
        st_all_saved(sp, 40)
        sp.wait_ge(dve_silu, 16)
        load_v(0)
        load_g(0)
        load_att(0)
        sp.dma_start(masks[:, :], c_mask).then_inc(mask_in, 16)
        def load_proj(j):
            for a, w in enumerate((w_pa, w_pb)):
                sp.dma_start(slot(w_raw, j, 8)[:, 4 * a:4 * a + 4, :], kview(w, cols(P * j, P), 0, 4)
                             ).then_inc(w_landed[j], 16)

        for j in range(6):
            sp.wait_ge(pe_cm, 14 + 2 * j)
            load_proj(j)

        with sp.Fori(0, NT - 1) as i:
            sp.wait_ge(pe_lv, i + 1)
            sp.wait_ge(act_dec, i + 1)
            sp.wait_ge(act_E7, i + 1)
            sp.wait_ge(dve_Xq, i + 1)
            load_qkb(i + 1)
            sp.wait_ge(pe_sc, 2 * i + 2)
            load_att(i + 1)
            sp.wait_ge(pe_gate, 4 * i + 2)
            load_gate(i + 1, 0)
            sp.wait_ge(pe_o, i + 1)
            load_v(i + 1)
            sp.wait_ge(pe_PV, i + 1)
            load_vwin(i + 1)
            sp.wait_ge(pe_gate, 4 * i + 4)
            load_gate(i + 1, 1)
            sp.wait_ge(dve_oa, i + 1)
            load_g(i + 1)
        sp.wait_ge(pe_gate, 4 * NT - 2)
        load_proj(6)
        sp.wait_ge(pe_gate, 4 * NT)
        load_proj(7)

        sp.wait_ge(oa_saved, 16 * NT)
        sp.wait_ge(ob_saved, 16 * NT)
        sp.wait_ge(pe_obT, NT)
        sp.wait_ge(act_ob, NT)
        sp.wait_ge(dve_oa, NT)
        for i in range(2):
            sp.wait_ge(gate_saved[i], 16 * 2 * NT)
        for H in range(2):
            for a in range(2):
                sp.dma_start(mix_raw[:, a, 4 * H:4 * H + 4, :],
                             mix_d[a, 4 * H:4 * H + 4].rearrange("q p n -> p q n")).then_inc(mix_in[2 * H + a], 16)
        for j in range(KT):
            for H in range(2):
                n = 2 * j + H
                if n >= 2:
                    sp.wait_ge(dve_m, n - 1)
                sp.dma_start(gt[:, n % 2, :, :],
                             gate_d[:, j, :, HALF * H:HALF * (H + 1)].rearrange("a p n -> p a n")
                             ).then_inc(gt_in[n % 2], 16)
            sp.wait_ge(pe_mix, 2 * j + 2)
            c, g = divmod(j, 4)
            load_weights(kview(w_o, cols(HALF * c, HALF), 2 * g, 2), j, 2).then_inc(w_landed[j], 16)

        sp.wait_ge(dve_m, 16)
        sp.wait_ge(act_mhi, 16)
        sp.wait_ge(dve_mlo, 16)
        sp.dma_start(hb[:, :], h_d[0]).then_inc(hb_in, 16)
        sp.dma_start(l1g[:, :], ln1_g[0].partition_broadcast(P)).then_inc(l1_in, 16)
        sp.dma_start(l1b[:, :], ln1_b[0].partition_broadcast(P)).then_inc(l1_in, 16)
        for t in range(1, NT):
            sp.wait_ge(pe_h1T, t)
            sp.wait_ge(h1_saved, 16 * t)
            sp.dma_start(hb[:, :], h_d[t]).then_inc(hb_in, 16)

        def load_block(b, prior):
            for f in range(FT):
                if prior is None:
                    sp.wait_ge(pe_wo, 2 * NT - 1)
                else:
                    sp.wait_ge(pe_up, 8 * prior + 2 * f + 2)
                load_weights(w_up[:, bass.ds(HALF * b + P * f, P)].rearrange("(k p) n -> p k n", p=P), f, 8
                             ).then_inc(w_landed[f], 16)
            for c in range(2):
                for g in range(2):
                    s = 4 + 2 * c + g
                    if prior is None:
                        sp.wait_ge(pe_wo, 2 * NT)
                    else:
                        sp.wait_ge(pe_down, 16 * prior + 15 + c)
                    load_weights(w_down[bass.ds(HALF * b + 2 * P * g, 2 * P), HALF * c:HALF * (c + 1)]
                                 .rearrange("(k p) n -> p k n", p=P), s, 2).then_inc(w_landed[s], 16)

        load_block(0, None)
        sp.wait_ge(pe_wo, 2 * NT)
        sp.wait_ge(h1_saved, 16 * NT)
        sp.dma_start(y[:, :, :], h1_d.rearrange("t p n -> p t n")).then_inc(y_in, 16)
        with sp.Fori(0, NBLK - 1) as i:
            load_block(i + 1, i)
        sp.wait_ge(dve_ulo, 8 * NBLK)
        sp.wait_ge(act_uhi, 8 * NBLK)
        sp.dma_start(l2g[:, :], ln2_g[0].partition_broadcast(P)).then_inc(l2_in, 16)
        sp.dma_start(l2b[:, :], ln2_b[0].partition_broadcast(P)).then_inc(l2_in, 16)
        for t in range(NT):
            sp.wait_ge(dve_out, t + 1)
            sp.dma_start(out[P * t:P * (t + 1), :], y[:, t, :]).then_inc(out_saved, 16)
        sp.wait_ge(out_saved, 16 * NT)

    landed_before_D = [48] * 6 + [16 * (2 + NT)] * 2

    @block.gpsimd
    def _(pool):
        seq = Tally(pool_seq)

        def link(ins):
            ins.then_inc(pool_seq, 1)
            seq.n += 1
            pool.wait_ge(pool_seq, seq.now())

        def split(n, s, uses):
            pool.wait_ge(w_landed[s], uses)
            passed(pool, pool_passed, uses)
            nc.gpsimd.tensor_scalar(w_hi[:, s, :], w_raw[:, s, :], 1.0, 1.0, ALU.mult, ALU.mult).then_inc(w_split, 1)
            pool.wait_ge(w_split, 2 * n + 1)
            nc.gpsimd.tensor_tensor(w_lo[:, s, :], w_raw[:, s, :], w_hi[:, s, :].bitcast(F32), ALU.subtract
                                    ).then_inc(w_split, 1)

        def inv_sqrt(dst, src, eps, rows, scale=1.0):
            link(nc.gpsimd.tensor_scalar(dst, src, scale, eps, ALU.mult, ALU.add))
            return nc.gpsimd.tensor_tensor(dst, dst, neghalf[0:rows, 0:dst.shape[1]], ALU.pow)

        link(nc.gpsimd.memset(neghalf[:, :], -0.5))
        nc.gpsimd.memset(zero[:, :], 0.0).then_inc(pool_const, 1)
        for n in range(2):
            split(n, n, 16)
        for t in range(NT + 1):
            rows = P if t < NT else META
            pool.wait_ge(dve_stats, t + 1)
            if t >= 2:
                pool.wait_ge(dve_h, t - 1)
            inv_sqrt(rstd[0:rows, t % 2, 0:1], mv[0:rows, t % 2, 1:2], LN_EPS, rows).then_inc(pool_rstd, 1)
            if t < 6:
                split(t + 2, t + 2, 16)
        for n in range(SLOTS, N_C):
            split(n, n % SLOTS, 16 * (n // SLOTS + 1))

        def decays(p, first):
            pool.wait_ge(qkb_in, 16 * (p + 1))
            if first:
                pool.wait_ge(dve_silu, 16)
                st_all_saved(pool, 40)
                pool.wait_ge(b_saved, 64)
            else:
                pool.wait_ge(pe_lv, p)
                pool.wait_ge(pe_kdT, p)
            for n, h in enumerate(LEVELS):
                b = pin[:, 2, :].rearrange("p (q h) -> p q h", h=2 * h)
                d = X[:, n, :].rearrange("p (q h) -> p q h", h=2 * h)
                mid = b[:, :, h - 1:h].to_broadcast([P, HALF // (2 * h), h])
                nc.gpsimd.tensor_tensor(d[:, :, 0:h], mid, b[:, :, 0:h], ALU.subtract).then_inc(pool_D, 1)
                nc.gpsimd.tensor_tensor(d[:, :, h:2 * h], b[:, :, h:2 * h], mid, ALU.subtract).then_inc(pool_D, 1)
            b = pin[:, 2, :].rearrange("p (q h) -> p q h", h=CHUNK)
            nc.gpsimd.tensor_tensor(X[:, KD, :].rearrange("p (q h) -> p q h", h=CHUNK),
                                    b[:, :, CHUNK - 1:CHUNK].to_broadcast([P, 2 * HEADS, CHUNK]), b, ALU.subtract
                                    ).then_inc(pool_D, 1)

        def pair(p, last):
            if not last:
                decays(p + 1, False)
            pool.wait_ge(act_prob, 2 * p + 2)
            seen(pool, pe_PT, 3 * p)
            passed(pool, pool_passed, p)
            nc.gpsimd.tensor_scalar(probm[:, :].rearrange("p (h m) -> p h m", m=META), prob[:, :, 0:META], 1.0, 1.0,
                                    ALU.mult, ALU.mult).then_inc(pool_probm, 1)
            if not last:
                split(N_C + 2 * p + 2, SLOT_GA, 16 * (p + 4))
            pool.wait_ge(pool_const, 1)
            pool.wait_ge(dve_osum, p + 1)
            seen(pool, dve_on, p)
            passed(pool, pool_passed, p)
            inv_sqrt(orms[:, :], osum[:, :], RMS_EPS, P, 1.0 / P).then_inc(pool_orms, 1)
            if not last:
                split(N_C + 2 * p + 3, SLOT_GB, 16 * (p + 4))

        split(N_C, SLOT_GA, 48)
        split(N_C + 1, SLOT_GB, 48)
        decays(0, True)
        pair(0, False)
        seq.begin(None, 0)
        with pool.Fori(0, NT - 2) as i:
            seq.begin(i, 1)
            pair(i + 1, False)
        seq.end(NT - 2)
        pair(NT - 1, True)
        for j in range(8):
            split(N_D + j, j, landed_before_D[j] + 32)
        for j in range(8):
            split(N_E + j, j, landed_before_D[j] + 48)
        def block_split(b):
            for s in range(8):
                split(N_F + 8 * b + s, s, landed_before_D[s] + 64 + 16 * b)

        for t in range(NT):
            pool.wait_ge(dve_r, t + 1)
            inv_sqrt(rstd[:, t % 2, 0:1], mv[:, t % 2, 1:2], LN_EPS, P).then_inc(pool_rstd, 1)
        block_split(0)
        with pool.Fori(0, NBLK - 1) as i:
            block_split(i + 1)
        for t in range(NT):
            pool.wait_ge(dve_r, NT + t + 1)
            inv_sqrt(rstd[:, t % 2, 0:1], mv[:, t % 2, 1:2], LN_EPS, P).then_inc(pool_rstd, 1)

    @block.tensor
    def _(pe):
        def mm(o, lhsT, rhs, start, stop):
            return nc.tensor.matmul(o, lhsT, rhs, start=start, stop=stop, skip_group_check=True)

        def gemm_w_stationary(o, s, k_of, moving_hi, moving_lo, ks, first=True, last=True):
            ins = None
            for n, k in enumerate(ks):
                a, z = first and n == 0, last and n == len(ks) - 1
                wh, wl = slot(w_hi, s, k_of)[:, k, :], slot(w_lo, s, k_of)[:, k, :]
                mm(o, wh, moving_hi(k), a, False)
                mm(o, wh, moving_lo(k), False, False)
                ins = mm(o, wl, moving_hi(k), False, z)
            return ins

        def gemm_w_moving(o, s0, per, still_hi, still_lo, nk):
            ins = None
            for k in range(nk):
                s, kk = s0 + k // per, k % per
                wh, wl = slot(w_hi, s, per)[:, kk, :], slot(w_lo, s, per)[:, kk, :]
                mm(o, still_hi(k), wh, k == 0, False)
                mm(o, still_hi(k), wl, False, False)
                ins = mm(o, still_lo(k), wh, False, k == nk - 1)
            return ins

        pe.wait_ge(tab_in, 48)

        def transpose_h(t):
            rows = P if t < NT else META
            pe.wait_ge(dve_h, t + 1)
            if t >= 2:
                pe.wait_ge(act_hi, t - 1)
                pe.wait_ge(dve_lo, t - 1)
            b0 = 4 + 2 * (t % 2)
            for k in range(KT):
                last = nc.tensor.transpose(ps[:, b0 + k // 4, P * (k % 4):P * (k % 4) + rows],
                                           xb[0:rows, t % 3, P * k:P * (k + 1)], ident[0:rows, 0:rows])
            last.then_inc(pe_hT, 1)

        def h_part(part, t):
            rows = P if t < NT else META
            return lambda k: part[:, k, P * t:P * t + rows]

        def token_unit(u, t, s0, per, n, width):
            rows = P if t < NT else META
            if u >= 2:
                pe.wait_ge(act_tm, u - 1)
            pe.wait_ge(w_split, 2 * n)
            o = ps[0:rows, u % 2, 0:width]
            ins = gemm_w_moving(o, s0, per, h_part(hT_hi, t), h_part(hT_lo, t), KT)
            ins.then_inc(pe_tm, 1)

        transpose_h(0)
        for t in range(NT + 1):
            if t < NT:
                transpose_h(t + 1)
            pe.wait_ge(act_hi, t + 1)
            pe.wait_ge(dve_lo, t + 1)
            token_unit(t, t, 0, 2, 4, HALF)

        def transpose_q(t):
            pe.wait_ge(dve_rope, t + 1)
            if t >= 2:
                pe.wait_ge(act_qT, t - 1)
            for h in range(HEADS):
                last = nc.tensor.transpose(ps[:, 4 + t % 2, P * h:P * (h + 1)], qtm[:, t % 2, P * h:P * (h + 1)],
                                           ident[:, :])
            last.then_inc(pe_qT, 1)

        for t in range(NT):
            token_unit(9 + t, t, 4, 2, 8, HALF)
            if t >= 1:
                transpose_q(t - 1)

        def transpose_k(t):
            rows = P if t < NT else META
            pe.wait_ge(dve_krope, t + 1)
            if t >= 2:
                pe.wait_ge(act_kT, t - 1)
            for j in range(2):
                last = nc.tensor.transpose(ps[:, 6 + t % 2, P * j:P * j + rows],
                                           ktm[0:rows, t % 2, j, :, :].rearrange("p a b -> p (a b)"),
                                           ident[0:rows, 0:rows])
            last.then_inc(pe_kT, 1)

        for t in range(NT + 1):
            token_unit(17 + t, t, 0, 4, 10, 256)
            if t == 0:
                transpose_q(NT - 1)
            else:
                transpose_k(t - 1)

        def channel_unit(v, n):
            H = v % 2
            if v < 2:
                pe.wait_ge(act_tm, 26)
            elif 4 <= v < 12:
                pe.wait_ge(act_cm, v - 3)
            elif v >= 12:
                pe.wait_ge(dve_silu, v - 11)
            pe.wait_ge(w_split, 2 * (n + 1))
            ins = gemm_w_stationary(ps[:, v % 4, :], n % SLOTS, 8,
                                    lambda k: hT_hi[:, k, HALF * H:HALF * (H + 1)],
                                    lambda k: hT_lo[:, k, HALF * H:HALF * (H + 1)], range(KT))
            ins.then_inc(pe_cm, 1)

        for hd in range(HEADS):
            n = 10 + hd
            channel_unit(2 * hd, n)
            channel_unit(2 * hd + 1, n)
            if hd == 0:
                transpose_k(NT)
                pe.wait_ge(act_hi, NT + 1)
            if hd >= 2:
                pe.wait_ge(act_fm, hd - 1)
            bank = 4 + hd % 2
            if hd < 2:
                pe.wait_ge(act_qT, 7 + hd)
            ins = gemm_w_stationary(ps[:, bank, 0:META], n % SLOTS, 8, lambda k: hT_hi[:, k, T:TA],
                                    lambda k: hT_lo[:, k, T:TA], range(KT))
            ins.then_inc(pe_fm, 1)
        for v in range(8, 24):
            channel_unit(v, 10 + v // 2)
            if v == 15:
                pe.wait_ge(dve_kdm, 1)
                pe.wait_ge(act_kT, NT + 1)
                for hd in range(HEADS):
                    last = nc.tensor.transpose(ps[0:META, 6, P * hd:P * (hd + 1)], dmeta[:, hd, :], ident[:, :])
                last.then_inc(pe_meta, 1)
            if v == 17:
                pe.wait_ge(act_meta, 2)
                for hd in range(HEADS):
                    last = mm(ps[:, 7, P * hd:P * (hd + 1)], qtm[0:META, 0, P * hd:P * (hd + 1)],
                              vmeta[:, P * hd:P * (hd + 1)], True, True)
                last.then_inc(pe_meta, 1)

        def gate_unit(p, u, ks, first, last):
            a, H = divmod(u, 2)
            s = (SLOT_GA, SLOT_GB)[a]
            if first:
                pe.wait_ge(w_split, 2 * (N_C + 1 + 2 * p + a))
                if isinstance(p, int) and p == 0 and u < 2:
                    pe.wait_ge(dve_silu, 13 + u)
                else:
                    pe.wait_ge(act_gate, 4 * p + u - 1)
            ins = gemm_w_stationary(ps[:, H, :], s, 8, lambda k: hT_hi[:, k, HALF * H:HALF * (H + 1)],
                                    lambda k: hT_lo[:, k, HALF * H:HALF * (H + 1)], ks, first, last)
            if last:
                ins.then_inc(pe_gate, 1)

        def pair(p, first):
            one = p + 1
            pe.wait_ge(dve_X, one)
            if first:
                pe.wait_ge(dve_silu, 16)
                pe.wait_ge(act_meta, 3)
                pe.wait_ge(act_fm, 4)
                pe.wait_ge(act_kT, NT + 1)
            else:
                pe.wait_ge(act_PT, 3 * p)
                pe.wait_ge(act_prob, 2 * p)
            for hd in range(HEADS):
                cs = slice(P * hd, P * (hd + 1))
                for n, h in enumerate(LEVELS):
                    right = X[:, n, cs].rearrange("p (q h) -> p q h", h=2 * h)[:, :, h:2 * h]
                    mm(ps[:, 2 + hd, CHUNK * n:CHUNK * (n + 1)], X[:, n, cs], right, True, True)
                last = mm(ps[:, 2 + hd, 384:512], pin[:, 1, cs], pin[:, 0, cs], True, True)
            last.then_inc(pe_lv, 1)
            if not first:
                pe.wait_ge(act_ob, p)
            for hd in range(HEADS):
                last = nc.tensor.transpose(ps[:, 6, P * hd:P * (hd + 1)], X[:, KD, P * hd:P * (hd + 1)], ident[:, :])
            last.then_inc(pe_kdT, 1)
            gate_unit(p, 0, range(KT), True, True)
            pe.wait_ge(act_kdT, one)
            pe.wait_ge(v_in, 16 * one)
            if not first:
                pe.wait_ge(dve_oa, p)
            for c in range(2):
                rs = slice(CHUNK * c, CHUNK * (c + 1))
                for hd in range(HEADS):
                    cs = slice(P * hd, P * (hd + 1))
                    last = mm(ps[:, 7 - c, cs], kdT[rs, cs], pv_[rs, cs], True, True)
                last.then_inc(pe_U, 1)
            pe.wait_ge(q_in, 32 * one)
            for g in range(2):
                pe.wait_ge(dve_prod, 2 * p + g + 1)
                for hh in range(4):
                    h = 4 * g + hh
                    j, ds = h // 4, slice(64 * (h % 2), 64 * (h % 2) + 64)
                    bank, off = 2 + 2 * g + hh % 2, 256 * (hh // 2)
                    mm(ps[:, bank, off:off + META], pqT[ds, h // 2, :], kTm[ds, j, :], True, True)
                    for c in range(2):
                        o = ps[CHUNK * c:CHUNK * (c + 1), bank, off + META:off + META + P]
                        masked = first and c == 0
                        last = mm(o, pqT[ds, h // 2, CHUNK * c:CHUNK * (c + 1)],
                                  kwin[ds, j, CHUNK * c:CHUNK * c + P], True, not masked)
                        if masked:
                            row = slice(64 * (h % 2), 64 * (h % 2) + 1)
                            last = mm(o, ones[row, :], negm[row, :], False, True)
                last.then_inc(pe_sc, 1)
            gate_unit(p, 1, range(KT), True, True)
            pe.wait_ge(dve_A, one)
            pe.wait_ge(dve_S, 2 * p + 1)
            pe.wait_ge(dve_Xq, one)
            for hd in range(HEADS):
                cs = slice(P * hd, P * (hd + 1))
                mm(ps[:, 7, cs], Amat[:, hd, :], pv_[:, cs], True, False)
                for c in range(2):
                    last = mm(ps[CHUNK * c:CHUNK * (c + 1), 7, cs],
                              X[:, QE, P * hd + CHUNK * c:P * hd + CHUNK * (c + 1)], (S0, S1)[c][:, hd, :],
                              False, True)
            last.then_inc(pe_o, 1)
            gate_unit(p, 2, range(KT), True, True)
            for g in range(2):
                pe.wait_ge(act_prob, 2 * p + g + 1)
                for hh in range(4):
                    last = nc.tensor.transpose(ps[:, 2 + 2 * g, P * hh:P * (hh + 1)],
                                               prob[:, 4 * g + hh, META:META + P], ident[:, :])
                last.then_inc(pe_PT, 1)
            pe.wait_ge(pool_probm, one)
            nc.tensor.transpose(ps[:, 3, 0:P], probm[:, :], ident[:, :]).then_inc(pe_PT, 1)
            gate_unit(p, 3, range(4), True, False)
            pe.wait_ge(act_PT, 3 * p + 3)
            pe.wait_ge(vw_in, 32 * one)
            pe.wait_ge(dve_S, 2 * p + 2)
            if first:
                pe.wait_ge(vmb_in, 16 * QH)
            mm(ps[:, 6, :], probmT[:, :], vmb[:, :], True, False)
            for h in range(QH):
                for c in range(2):
                    last = mm(ps[CHUNK * c:CHUNK * (c + 1), 6, 64 * h:64 * (h + 1)],
                              probT[:, h, CHUNK * c:CHUNK * (c + 1)], vwin[:, c, 64 * (h // 4):64 * (h // 4) + 64],
                              False, True)
            last.then_inc(pe_PV, 1)
            gate_unit(p, 3, range(4, KT), False, True)
            pe.wait_ge(dve_on, one)
            for hd in range(HEADS):
                last = nc.tensor.transpose(ps[:, 7, P * hd:P * (hd + 1)], o_sb[:, hd, :], ident[:, :])
            last.then_inc(pe_oT, 1)
            pe.wait_ge(dve_ob, one)
            for hd in range(HEADS):
                last = nc.tensor.transpose(ps[:, 6, P * hd:P * (hd + 1)],
                                           ob[:, 2 * hd:2 * hd + 2, :].rearrange("p a b -> p (a b)"), ident[:, :])
            last.then_inc(pe_obT, 1)

        pair(0, True)
        with pe.Fori(1, NT) as i:
            pair(i, False)

        for j in range(KT):
            pe.wait_ge(w_split, 2 * (N_D + j + 1))
            for H in range(2):
                n = 2 * j + H
                if j == 0:
                    for a in range(2):
                        pe.wait_ge(act_mixhi, 2 * H + a + 1)
                        pe.wait_ge(dve_mixlo, 2 * H + a + 1)
                if n < 4:
                    if n == 0:
                        pe.wait_ge(act_gate, 4 * NT)
                        pe.wait_ge(act_ob, NT)
                        pe.wait_ge(dve_oa, NT)
                        pe.wait_ge(act_PT, 3 * NT)
                else:
                    pe.wait_ge(dve_m, n - 3)
                for a in range(2):
                    ins = gemm_w_stationary(ps[:, 2 * (n % 4) + a, :], j, 8,
                                            lambda k: mix_hi[:, a, 4 * H:4 * H + 4, P * (k % 4):P * (k % 4) + P],
                                            lambda k: mix_lo[:, a, 4 * H:4 * H + 4, P * (k % 4):P * (k % 4) + P],
                                            range(4 * a, 4 * a + 4))
                ins.then_inc(pe_mix, 1)

        def transpose_h1(t):
            pe.wait_ge(dve_h1, t + 1)
            if t >= 2:
                pe.wait_ge(act_h1hi, t - 1)
                pe.wait_ge(dve_h1lo, t - 1)
            b0 = 4 + 2 * (t % 2)
            for k in range(KT):
                last = nc.tensor.transpose(ps[:, b0 + k // 4, P * (k % 4):P * (k % 4 + 1)], hb[:, P * k:P * (k + 1)],
                                           ident[:, :])
            last.then_inc(pe_h1T, 1)

        pe.wait_ge(dve_m, 16)
        pe.wait_ge(act_mhi, 16)
        pe.wait_ge(dve_mlo, 16)
        for t in range(NT):
            if t >= 2:
                pe.wait_ge(dve_r, t - 1)
            for c in range(2):
                pe.wait_ge(w_split, 2 * (N_E + 4 * c + 4))
                ins = gemm_w_moving(ps[:, 2 * (t % 2) + c, :], 4 * c, 2, lambda k: mT_hi[:, k, P * t:P * (t + 1)],
                                    lambda k: mT_lo[:, k, P * t:P * (t + 1)], KT)
                ins.then_inc(pe_wo, 1)
            if t >= 1:
                transpose_h1(t - 1)
        transpose_h1(NT - 1)

        def ff_block(b, first):
            for f in range(FT):
                for H in range(2):
                    u = 2 * f + H
                    if u < 2 and first and H == 0:
                        pe.wait_ge(act_h1hi, 4)
                        pe.wait_ge(dve_h1lo, 4)
                        pe.wait_ge(dve_r, NT)
                    if u == 1 and first:
                        pe.wait_ge(act_h1hi, NT)
                        pe.wait_ge(dve_h1lo, NT)
                    if u >= 4:
                        pe.wait_ge(dve_us, 8 * b + u - 3)
                    elif not first:
                        pe.wait_ge(dve_us, 8 * b + u - 3)
                    pe.wait_ge(w_split, 2 * (N_F + 8 * b + f + 1))
                    ins = gemm_w_stationary(ps[:, u % 4, :], f, 8, lambda k: h1T_hi[:, k, HALF * H:HALF * (H + 1)],
                                            lambda k: h1T_lo[:, k, HALF * H:HALF * (H + 1)], range(KT))
                    ins.then_inc(pe_up, 1)
            for t in range(NT):
                if t == 0:
                    pe.wait_ge(act_uhi, 8 * b + 7)
                    pe.wait_ge(dve_ulo, 8 * b + 7)
                if t == 4:
                    pe.wait_ge(act_uhi, 8 * b + 8)
                    pe.wait_ge(dve_ulo, 8 * b + 8)
                for c in range(2):
                    n = 2 * t + c
                    if first and n < 4:
                        pe.wait_ge(act_h1hi, NT)
                        pe.wait_ge(dve_h1lo, NT)
                    else:
                        pe.wait_ge(dve_y, 16 * b + n - 3)
                    pe.wait_ge(w_split, 2 * (N_F + 8 * b + 6 + 2 * c))
                    ins = gemm_w_moving(ps[:, 4 + n % 4, :], 4 + 2 * c, 2, lambda k: u_hi[:, k, P * t:P * (t + 1)],
                                        lambda k: u_lo[:, k, P * t:P * (t + 1)], FT)
                    ins.then_inc(pe_down, 1)

        ff_block(0, True)
        with pe.Fori(1, NBLK) as i:
            ff_block(i, False)

    @block.scalar
    def _(act):
        fn = nc.scalar.activation

        def copy(dst, src):
            return fn(dst, src, ACT.Copy)

        def pair_view(idx, t):
            return pair_d[t, :, idx, :]

        def head_tokens(idx, hd, H):
            return pair_d[4 * H:4 * H + 4, :, idx, P * hd:P * (hd + 1)].rearrange("q p n -> p q n")


        def hT_high(t):
            n = P if t < NT else META
            act.wait_ge(pe_hT, t + 1)
            b0 = 4 + 2 * (t % 2)
            src = ps[:, b0:b0 + 2, :].rearrange("p b (k n) -> p (b k) n", n=P)[:, :, 0:n]
            copy(hT_hi[:, :, P * t:P * t + n], src).then_inc(act_hi, 1)

        def save_h(t):
            act.wait_ge(dve_h, t + 1)
            act.dma_start(h_d[t], xb[:, t % 3, :]).then_inc(h_saved[t % 3], 16)

        def save_st(idx, dst, made, count):
            act.wait_ge(made, count)
            act.dma_start(dst, st[:, idx % 6, :] if len(dst.shape) == 2 else as_pairs(st[:, idx % 6, :])
                          ).then_inc(st_saved[idx % 6], 16)

        save_h(0)
        hT_high(0)
        for t in range(NT + 1):
            if t < NT:
                if t + 1 < NT:
                    save_h(t + 1)
                hT_high(t + 1)
            act.wait_ge(pe_tm, t + 1)
            if t < NT:
                st_free(act, t)
                copy(st[:, t % 6, :], ps[:, t % 2, :]).then_inc(act_tm, 1)
            else:
                copy(vmeta[:, :], ps[0:META, t % 2, :]).then_inc(act_tm, 1)
            if t >= 1:
                save_st(t - 1, pair_view(3, t - 1), act_tm, t)
            if t == 2:
                act.wait_ge(dve_lb, 1)
                fn(lbe[:, :, :], lbl[:, :, :], ACT.Exp).then_inc(act_lb, 1)

        def qT_out(t):
            act.wait_ge(pe_qT, t + 1)
            st_free(act, 8 + t)
            copy(st[:, (8 + t) % 6, :], ps[:, 4 + t % 2, :]).then_inc(act_qT, 1)

        for t in range(NT):
            act.wait_ge(pe_tm, 10 + t)
            if t >= 2:
                act.wait_ge(pe_qT, t - 1)
            copy(qtm[:, t % 2, :], ps[:, (9 + t) % 2, :]).then_inc(act_tm, 1)
            if t >= 1:
                qT_out(t - 1)
            if t >= 2:
                save_st(8 + t - 2, pair_view(5, t - 2), act_qT, t - 1)

        def kT_out(t):
            act.wait_ge(pe_kT, t + 1)
            src = ps[:, 6 + t % 2, 0:2 * P].rearrange("p (j n) -> p j n", j=2)
            if t < NT:
                copy(kTs[:, t % 2, :, :], src).then_inc(act_kT, 1)
            else:
                copy(kTm[:, :, :], src[:, :, 0:META]).then_inc(act_kT, 1)

        def save_kv(t):
            act.wait_ge(act_kT, t + 1)
            c0 = CHUNK + P * t
            act.dma_start(kT_d[:, :, c0:c0 + P], kTs[:, t % 2, :, :]).then_inc(kv_saved[t % 2], 16)
            act.dma_start(vb_d[c0:c0 + P, :], vst[:, t % 2, :]).then_inc(kv_saved[t % 2], 16)

        for i in range(3):
            act.wait_ge(h_saved[i], (48, 48, 32)[i])
        for t in range(NT + 1):
            rows = P if t < NT else META
            act.wait_ge(pe_tm, 18 + t)
            if t >= 2:
                act.wait_ge(pe_kT, t - 1)
                act.wait_ge(kv_saved[t % 2], 32 * (t // 2))
            src = ps[0:rows, (17 + t) % 2, :]
            copy(ktm[0:rows, t % 2, :, 0, :], src[:, 0:P].rearrange("p (j d) -> p j d", j=2))
            copy(vst[0:rows, t % 2, :], src[:, P:2 * P]).then_inc(act_tm, 1)
            if t == 0:
                qT_out(NT - 1)
                save_st(8 + NT - 2, pair_view(5, NT - 2), act_qT, NT - 1)
            else:
                if t == 1:
                    save_st(8 + NT - 1, pair_view(5, NT - 1), act_qT, NT)
                kT_out(t - 1)
                save_kv(t - 1)

        for hd in range(HEADS):
            for H in range(2):
                v = 2 * hd + H
                act.wait_ge(pe_cm, v + 1)
                fn(fst[:, hd, HALF * H:HALF * (H + 1)], ps[:, v % 4, :], ACT.Sigmoid).then_inc(act_cm, 1)
                if v >= 1:
                    save_st(16 + v - 1, head_tokens(1, (v - 1) // 2, (v - 1) % 2), dve_k, v)
            if hd == 0:
                kT_out(NT)
            act.wait_ge(pe_fm, hd + 1)
            fn(fst[:, hd, T:TA], ps[:, 4 + hd % 2, 0:META], ACT.Sigmoid).then_inc(act_fm, 1)
        save_st(23, head_tokens(1, 3, 1), dve_k, 8)
        for hd in range(HEADS):
            act.wait_ge(dve_f, hd + 1)
            fn(fst[:, hd, :], fst[:, hd, :], ACT.Ln).then_inc(act_ln, 1)

        def silu_sigmoid(v):
            act.wait_ge(pe_cm, v + 1)
            seen(act, dve_silu, v - 9)
            fn(sg[:, v % 2, :], ps[:, v % 4, :], ACT.Sigmoid).then_inc(act_cm, 1)
            if v >= 9:
                w = v - 1
                save_st(16 + w, head_tokens(0 if w < 16 else 4, w // 2 % 4, w % 2), dve_silu, w - 7)

        for v in range(8, 24):
            silu_sigmoid(v)
            if v == 9:
                for hd in range(HEADS):
                    act.wait_ge(dve_scan, hd + 1)
                    act.dma_start(pair_d[:, :, 2, P * hd:P * (hd + 1)].rearrange("q p n -> p q n"),
                                  as_pairs(fst[:, hd, 0:T])).then_inc(b_saved, 16)
            if v == 12:
                act.wait_ge(dve_meta, 1)
                fn(dmeta[:, :, :], dmeta[:, :, :], ACT.Exp).then_inc(act_meta, 1)
            if v == 16:
                act.wait_ge(pe_meta, 1)
                copy(qtm[0:META, 0, :], ps[0:META, 6, :]).then_inc(act_meta, 1)
            if v == 18:
                act.wait_ge(pe_meta, 2)
                copy(S0[:, :, :].rearrange("p h n -> p (h n)"), ps[:, 7, :]).then_inc(act_meta, 1)
        save_st(39, head_tokens(4, 3, 1), dve_silu, 16)

        def exp_decays(p):
            act.wait_ge(pool_D, 13 * (p + 1))
            fn(X[:, 0:NL + 1, :], X[:, 0:NL + 1, :], ACT.Exp).then_inc(act_E, 1)

        def exp_qe(p):
            act.wait_ge(qkb_in, 16 * (p + 1))
            seen(act, pe_o, p)
            fn(X[:, QE, :], pin[:, 2, :], ACT.Exp).then_inc(act_E7, 1)

        def chunk_decay(p):
            seen(act, dve_S, 2 * p)
            b = pin[:, 2, :].rearrange("p (h c n) -> p h c n", h=HEADS, c=2)
            fn(decay[:, :, :], b[:, :, :, CHUNK - 1], ACT.Exp).then_inc(act_dec, 1)

        def gate_out(p, u):
            a, H = divmod(u, 2)
            act.wait_ge(pe_gate, 4 * p + u + 1)
            seen(act, gate_saved[H], 32 * p + 16 * a)
            act.wait_ge(small_in, 64)
            passed(act, act_passed, p)
            fn(gst[:, H, :], ps[:, H, :], ACT.Identity, bias=bgate[:, a, bass.ds(p, 1)]).then_inc(act_gate, 1)

        def save_gate(p, u):
            a, H = divmod(u, 2)
            act.wait_ge(act_gate, 4 * p + u + 1)
            act.dma_start(gate_d[a, bass.ds(p, 1), :, HALF * H:HALF * (H + 1)].rearrange("a p n -> p (a n)"),
                          gst[:, H, :]).then_inc(gate_saved[H], 16)

        def pair(p, first, last):
            one = p + 1
            act.wait_ge(pe_kdT, one)
            copy(kdT[:, :], ps[:, 6, :]).then_inc(act_kdT, 1)
            gate_out(p, 0)
            for g in range(2):
                act.wait_ge(dve_nb, 2 * p + g + 1)
                if not first:
                    act.wait_ge(pool_probm, p)
                    act.wait_ge(dve_ob, p)
                for hh in range(4):
                    h = 4 * g + hh
                    bank, off = 2 + 2 * g + hh % 2, 256 * (hh // 2)
                    ins = fn(prob[:, h, :], ps[:, bank, off:off + META + P], ACT.Exp, bias=negmax[:, h:h + 1],
                             scale=SCALE, accum_out=rowsum[:, h:h + 1])
                ins.then_inc(act_prob, 1)
            save_gate(p, 0)
            act.wait_ge(dve_snk, one)
            fn(sinkexp[:, :], sinkexp[:, :], ACT.Exp).then_inc(act_es, 1)
            if not last:
                exp_decays(p + 1)
            gate_out(p, 1)
            act.wait_ge(pe_o, one)
            copy(o_sb[:, :, :].rearrange("p h n -> p (h n)"), ps[:, 7, :]).then_inc(act_o, 1)
            save_gate(p, 1)
            if not last:
                exp_qe(p + 1)
            gate_out(p, 2)
            if not last:
                chunk_decay(p + 1)
            for g in range(2):
                act.wait_ge(pe_PT, 3 * p + g + 1)
                copy(probT[:, 4 * g:4 * g + 4, :].rearrange("p h n -> p (h n)"), ps[:, 2 + 2 * g, :]
                     ).then_inc(act_PT, 1)
            act.wait_ge(pe_PT, 3 * p + 3)
            copy(probmT[:, :], ps[:, 3, 0:P]).then_inc(act_PT, 1)
            save_gate(p, 2)
            gate_out(p, 3)
            act.wait_ge(dve_oa, one)
            act.dma_start(mix_d[0, bass.ds(p, 1)].rearrange("a p n -> p (a n)"), oast[:, :]).then_inc(oa_saved, 16)
            act.wait_ge(pe_obT, one)
            seen(act, ob_saved, 16 * p)
            copy(obst[:, :], ps[:, 6, :]).then_inc(act_ob, 1)
            save_gate(p, 3)
            act.wait_ge(act_ob, one)
            act.dma_start(mix_d[1, bass.ds(p, 1)].rearrange("a p n -> p (a n)"), obst[:, :]).then_inc(ob_saved, 16)

        exp_decays(0)
        exp_qe(0)
        chunk_decay(0)
        pair(0, True, False)
        with act.Fori(1, NT - 1) as i:
            pair(i, False, False)
        pair(NT - 1, False, True)

        for n in range(4):
            H, a = divmod(n, 2)
            act.wait_ge(mix_in[n], 16)
            copy(mix_hi[:, a, 4 * H:4 * H + 4, :], mix_raw[:, a, 4 * H:4 * H + 4, :]).then_inc(act_mixhi, 1)

        def m_high(n):
            j, H = divmod(n, 2)
            act.wait_ge(dve_m, n + 1)
            copy(mT_hi[:, j, HALF * H:HALF * (H + 1)], t1[:, :]).then_inc(act_mhi, 1)

        for n in range(16):
            act.wait_ge(gt_in[n % 2], 16 * (n // 2 + 1))
            fn(gt[:, n % 2, :, :], gt[:, n % 2, :, :], ACT.Sigmoid).then_inc(act_sig, 1)
            if n >= 1:
                m_high(n - 1)
        m_high(15)

        for t in range(NT):
            act.wait_ge(dve_h1, t + 1)
            act.dma_start(h1_d[t], hb[:, :]).then_inc(h1_saved, 16)
            act.wait_ge(pe_h1T, t + 1)
            b0 = 4 + 2 * (t % 2)
            copy(h1T_hi[:, :, P * t:P * (t + 1)],
                 ps[:, b0:b0 + 2, :].rearrange("p b (k n) -> p (b k) n", n=P)).then_inc(act_h1hi, 1)

        def u_high(b, u):
            f, H = divmod(u, 2)
            act.wait_ge(dve_us, 8 * b + u + 1)
            copy(u_hi[:, f, HALF * H:HALF * (H + 1)], us[:, u % 2, :]).then_inc(act_uhi, 1)

        def ff_block(b, first):
            for u in range(2 * FT):
                act.wait_ge(pe_up, 8 * b + u + 1)
                if not (first and u < 2):
                    act.wait_ge(dve_us, 8 * b + u - 1)
                elif u == 0:
                    act.wait_ge(h1_saved, 16 * NT)
                    act.wait_ge(dve_h1, NT)
                fn(ur[:, u % 2, :], ps[:, u % 4, :], ACT.Relu).then_inc(act_ur, 1)
                if u >= 1:
                    u_high(b, u - 1)
            u_high(b, 2 * FT - 1)

        ff_block(0, True)
        with act.Fori(1, NBLK) as i:
            ff_block(i, False)

    @block.vector
    def _(dve):
        seq = Tally(dve_seq)
        V = nc.vector

        def mark(ins):
            ins.then_inc(dve_seq, 1)
            seq.n += 1

        def settle():
            dve.wait_ge(dve_seq, seq.now())

        def link(ins):
            mark(ins)
            settle()

        def norm(t_, mean, r, g, b):
            link(V.scalar_tensor_tensor(t_, t_, mean, g, ALU.subtract, ALU.mult))
            return V.scalar_tensor_tensor(t_, t_, r, b, ALU.mult, ALU.add)

        def row_stats(t, tile, rows=P):
            mark(V.bn_stats(stats[0:rows, t % 2, 0, :], tile[:, 0:HALF]))
            link(V.bn_stats(stats[0:rows, t % 2, 1, :], tile[:, HALF:D]))
            return V.bn_aggr(mv[0:rows, t % 2, :], stats[0:rows, t % 2, :, :].rearrange("p a b -> p (a b)"))

        def stats_x(t):
            rows = P if t < NT else META
            dve.wait_ge(x_in[t % 3], 16 * (t // 3 + 1))
            row_stats(t, xb[0:rows, t % 3, :], rows).then_inc(dve_stats, 1)

        def norm_x(t):
            rows = P if t < NT else META
            dve.wait_ge(pool_rstd, t + 1)
            tile = xb[0:rows, t % 3, :]
            norm(tile, mv[0:rows, t % 2, 0:1], rstd[0:rows, t % 2, 0:1], lng[0:rows, :], lnb[0:rows, :]
                 ).then_inc(dve_h, 1)

        def hT_low(t):
            n = P if t < NT else META
            dve.wait_ge(act_hi, t + 1)
            b0 = 4 + 2 * (t % 2)
            src = ps[:, b0:b0 + 2, :].rearrange("p b (k n) -> p (b k) n", n=P)[:, :, 0:n]
            cs = slice(P * t, P * t + n)
            V.tensor_tensor(hT_lo[:, :, cs], src, hT_hi[:, :, cs].bitcast(F32), ALU.subtract).then_inc(dve_lo, 1)

        stats_x(0)
        mark(V.memset(vmb[:, :], 0.0))
        mark(V.memset(negm[:, 0:CHUNK], NEG))
        mark(V.memset(negm[:, CHUNK:P], 0.0))
        mark(V.memset(yscale[:, 0:1], ALPHA))
        mark(V.memset(yscale[:, 1:NBLK], 1.0))
        V.memset(ones[:, :], 1.0).then_inc(dve_const, 1)
        dve.wait_ge(tab_in, 48)
        for t in range(NT + 1):
            if t < NT:
                stats_x(t + 1)
            norm_x(t)
            if t >= 1:
                hT_low(t - 1)
            if t == 2:
                dve.wait_ge(small_in, 64)
                link(V.tensor_tensor(lbm[:, :], lbl[:, 0, :], lbl[:, 1, :], ALU.max))
                mark(V.tensor_tensor(lbl[:, 0, :], lbl[:, 0, :], lbm[:, :], ALU.subtract))
                V.tensor_tensor(lbl[:, 1, :], lbl[:, 1, :], lbm[:, :], ALU.subtract).then_inc(dve_lb, 1)
                link(V.tensor_scalar(negsink[:, :], sinks[:, :], -1.0, None, ALU.mult))
            if t == 4:
                dve.wait_ge(act_lb, 1)
                link(V.tensor_tensor(lbm[:, :], lbe[:, 0, :], lbe[:, 1, :], ALU.add))
                link(V.reciprocal(lbm[:, :], lbm[:, :]))
                mark(V.tensor_tensor(lb[:, :], lbe[:, 0, :], lbm[:, :], ALU.mult))
                link(V.tensor_tensor(oml[:, :], lbe[:, 1, :], lbm[:, :], ALU.mult))
                mark(V.tensor_scalar(noml[:, :], oml[:, :], -1.0, None, ALU.mult))
        hT_low(NT)
        dve.wait_ge(dve_h, NT + 1)
        link(V.memset(scanmask[:, :], 1.0))
        link(V.memset(scanmask[:, 0:T + 1:CHUNK], 0.0))

        def rotate(t, rows, heads, nh):
            x1, x2 = heads[:, :, 0:8], heads[:, :, 8:16]
            cos = rope[0:rows, t, 0:1, :].to_broadcast([rows, nh, 8])
            sin = rope[0:rows, t, 1:2, :].to_broadcast([rows, nh, 8])
            tmp = [rtmp[0:rows, i, 0:8 * nh].rearrange("p (h d) -> p h d", d=8) for i in range(4)]
            for o, (a, b) in zip(tmp, ((x1, cos), (x2, sin), (x2, cos), (x1, sin))):
                mark(V.tensor_tensor(o, a, b, ALU.mult))
            settle()
            mark(V.tensor_tensor(x1, tmp[0], tmp[1], ALU.subtract))
            return V.tensor_tensor(x2, tmp[2], tmp[3], ALU.add)

        dve.wait_ge(rope_in, 16)
        for t in range(NT):
            dve.wait_ge(act_tm, 10 + t)
            seen(dve, dve_rope, t)
            rotate(t, P, qtm[:, t % 2, :].rearrange("p (h d) -> p h d", d=64), QH).then_inc(dve_rope, 1)
        dve.wait_ge(dve_rope, NT)
        for t in range(NT + 1):
            rows = P if t < NT else META
            dve.wait_ge(act_tm, 18 + t)
            seen(dve, dve_krope, t)
            link(rotate(t, rows, ktm[0:rows, t % 2, :, 0, :], 2))
            V.tensor_copy(ktm[0:rows, t % 2, :, 1, :], ktm[0:rows, t % 2, :, 0, :]).then_inc(dve_krope, 1)

        for hd in range(HEADS):
            o, no = oml[:, hd:hd + 1], noml[:, hd:hd + 1]
            for H in range(2):
                v = 2 * hd + H
                idx = 16 + v
                dve.wait_ge(act_cm, v + 1)
                st_free(dve, idx)
                V.tensor_scalar(st[:, idx % 6, :], fst[:, hd, HALF * H:HALF * (H + 1)], no, o, ALU.mult, ALU.add
                                ).then_inc(dve_k, 1)
            dve.wait_ge(act_fm, hd + 1)
            mark(V.tensor_scalar(kmeta[:, hd, :], fst[:, hd, T:TA], no, o, ALU.mult, ALU.add))
            dve.wait_ge(dve_k, 2 * hd + 2)
            settle()
            link(V.tensor_scalar(fst[:, hd, :], fst[:, hd, :], o, lb[:, hd:hd + 1], ALU.mult, ALU.add))
            V.tensor_scalar(fst[:, hd, :], fst[:, hd, :], TINY, None, ALU.max).then_inc(dve_f, 1)
        for hd in range(HEADS):
            dve.wait_ge(act_ln, hd + 1)
            V.tensor_tensor_scan(fst[:, hd, :], scanmask[:, :], fst[:, hd, :], 0.0, ALU.mult, ALU.add
                                 ).then_inc(dve_scan, 1)
        dve.wait_ge(dve_scan, HEADS)
        V.tensor_tensor(dmeta[:, :, :], fst[:, :, TA - 1:TA].to_broadcast([P, HEADS, META]), fst[:, :, T:TA],
                        ALU.subtract).then_inc(dve_meta, 1)
        for v in range(8, 24):
            idx = 16 + v
            dve.wait_ge(act_cm, v + 1)
            st_free(dve, idx)
            if v < 16:
                V.tensor_tensor(st[:, idx % 6, :], ps[:, v % 4, :], sg[:, v % 2, :], ALU.mult).then_inc(dve_silu, 1)
            else:
                hd = (v - 16) // 2
                V.scalar_tensor_tensor(st[:, idx % 6, :], ps[:, v % 4, :], normg[:, hd:hd + 1], sg[:, v % 2, :],
                                       ALU.mult, ALU.mult).then_inc(dve_silu, 1)
            if v == 12:
                dve.wait_ge(act_meta, 1)
                V.tensor_tensor(dmeta[:, :, :], dmeta[:, :, :], kmeta[:, :, :], ALU.mult).then_inc(dve_kdm, 1)

        def with_qk(p):
            dve.wait_ge(act_E, p + 1)
            dve.wait_ge(qkb_in, 16 * (p + 1))
            for n, h in enumerate(LEVELS):
                half = [z.rearrange("p (q h) -> p q h", h=2 * h) for z in (X[:, n, :], pin[:, 1, :], pin[:, 0, :])]
                left = [z[:, :, 0:h] for z in half]
                right = [z[:, :, h:2 * h] for z in half]
                mark(V.tensor_tensor(left[0], left[0], left[1], ALU.mult))
                mark(V.tensor_tensor(right[0], right[0], right[2], ALU.mult))
            V.tensor_tensor(X[:, KD, :], X[:, KD, :], pin[:, 1, :], ALU.mult).then_inc(dve_X, 1)
            dve.wait_ge(act_E7, p + 1)
            V.tensor_tensor(X[:, QE, :], X[:, QE, :], pin[:, 0, :], ALU.mult).then_inc(dve_Xq, 1)

        def new_state(p, c, src, dst, bank):
            for hd in range(HEADS):
                ins = V.scalar_tensor_tensor(dst[:, hd, :], src[:, hd, :], decay[:, hd, c:c + 1],
                                             ps[:, bank, P * hd:P * (hd + 1)], ALU.mult, ALU.add)
                if hd < HEADS - 1:
                    mark(ins)
            ins.then_inc(dve_S, 1)

        def pair(p, first, last):
            one = p + 1
            dve.wait_ge(pe_lv, one)
            if first:
                dve.wait_ge(mask_in, 16)
            for g in range(2):
                banks = ps[:, 2 + 2 * g:4 + 2 * g, :]
                mark(V.tensor_tensor(prod[:, 2 * g:2 * g + 2, :], banks[:, :, 0:384],
                                     masks[:, 0:384].rearrange("p (o n) -> p o n", o=1).to_broadcast([P, 2, 384]),
                                     ALU.mult))
                V.tensor_tensor(Amat[:, 2 * g:2 * g + 2, :], banks[:, :, 384:512],
                                masks[:, 384:512].rearrange("p (o n) -> p o n", o=1).to_broadcast([P, 2, P]),
                                ALU.mult).then_inc(dve_prod, 1)
            dve.wait_ge(dve_prod, 2 * p + 2)
            for n, h in enumerate(LEVELS):
                a = Amat[:, :, :].rearrange("p d (q h) -> p d q h", h=2 * h)[:, :, :, h:2 * h]
                pr = prod[:, :, CHUNK * n:CHUNK * (n + 1)].rearrange("p d (q h) -> p d q h", h=h)
                ins = V.tensor_tensor(a, a, pr, ALU.add)
                if n < NL - 1:
                    link(ins)
            ins.then_inc(dve_A, 1)
            dve.wait_ge(pe_U, 2 * p + 1)
            dve.wait_ge(act_dec, one)
            new_state(p, 0, S0, S1, 7)
            for g in range(2):
                dve.wait_ge(pe_sc, 2 * p + g + 1)
                sc = ps[:, 2 + 2 * g:4 + 2 * g, :].rearrange("p b (q n) -> p b q n", n=256)[:, :, :, 0:META + P]
                hs = slice(4 * g, 4 * g + 4)
                link(V.tensor_reduce(rowmax[:, hs].rearrange("p (q b) -> p b q", b=2), sc, AX, ALU.max))
                V.scalar_tensor_tensor(negmax[:, hs], rowmax[:, hs], -SCALE, negsink[:, hs], ALU.mult, ALU.min
                                       ).then_inc(dve_nb, 1)
            dve.wait_ge(dve_nb, 2 * p + 2)
            V.tensor_tensor(sinkexp[:, :], sinks[:, :], negmax[:, :], ALU.add).then_inc(dve_snk, 1)
            dve.wait_ge(act_o, one)
            link(V.tensor_tensor(osq[:, :, :], o_sb[:, :, :], o_sb[:, :, :], ALU.mult))
            V.tensor_reduce(osum[:, :], osq[:, :, :], AX, ALU.add).then_inc(dve_osum, 1)
            dve.wait_ge(pe_o, one)
            dve.wait_ge(pe_U, 2 * p + 2)
            dve.wait_ge(dve_S, 2 * p + 1)
            new_state(p, 1, S1, S0, 6)
            if not last:
                with_qk(p + 1)
            dve.wait_ge(pool_orms, one)
            V.tensor_tensor(o_sb[:, :, :], o_sb[:, :, :],
                            orms[:, :].rearrange("p (h o) -> p h o", o=1).to_broadcast([P, HEADS, P]), ALU.mult
                            ).then_inc(dve_on, 1)
            dve.wait_ge(act_es, one)
            dve.wait_ge(act_prob, 2 * p + 2)
            link(V.tensor_tensor(rden[:, :], rowsum[:, :], sinkexp[:, :], ALU.add))
            link(V.reciprocal(rden[:, :], rden[:, :]))
            dve.wait_ge(pe_PV, one)
            V.tensor_tensor(ob[:, :, :], ps[:, 6, :].rearrange("p (h d) -> p h d", d=64),
                            rden[:, :].rearrange("p (h o) -> p h o", o=1).to_broadcast([P, QH, 64]), ALU.mult
                            ).then_inc(dve_ob, 1)
            dve.wait_ge(pe_oT, one)
            dve.wait_ge(g_in, 16 * one)
            seen(dve, oa_saved, 16 * p)
            V.tensor_tensor(oast[:, :], ps[:, 7, :], pg[:, :], ALU.mult).then_inc(dve_oa, 1)

        with_qk(0)
        pair(0, True, False)
        per_pair = 2 + (NL - 1) + 3 + 2 + 1 + 3 + 2 * NL + 2
        with dve.Fori(0, NT - 2) as i:
            seq.begin(i, per_pair)
            pair(i + 1, False, False)
        seq.end(NT - 2)
        pair(NT - 1, False, True)

        for n in range(4):
            H, a = divmod(n, 2)
            dve.wait_ge(act_mixhi, n + 1)
            qs = slice(4 * H, 4 * H + 4)
            V.tensor_tensor(mix_lo[:, a, qs, :], mix_raw[:, a, qs, :], mix_hi[:, a, qs, :].bitcast(F32), ALU.subtract
                            ).then_inc(dve_mixlo, 1)
        for n in range(16):
            j, H = divmod(n, 2)
            dve.wait_ge(pe_mix, n + 1)
            dve.wait_ge(act_sig, n + 1)
            seen(dve, act_mhi, n)
            seen(dve, dve_mlo, n)
            mark(V.tensor_tensor(t1[:, :], ps[:, 2 * (n % 4), :], gt[:, n % 2, 0, :], ALU.mult))
            link(V.tensor_tensor(t2[:, :], ps[:, 2 * (n % 4) + 1, :], gt[:, n % 2, 1, :], ALU.mult))
            V.tensor_tensor(t1[:, :], t1[:, :], t2[:, :], ALU.add).then_inc(dve_m, 1)
            dve.wait_ge(act_mhi, n + 1)
            hs = slice(HALF * H, HALF * (H + 1))
            V.tensor_tensor(mT_lo[:, j, hs], t1[:, :], mT_hi[:, j, hs].bitcast(F32), ALU.subtract
                            ).then_inc(dve_mlo, 1)

        for t in range(NT):
            dve.wait_ge(hb_in, 16 * (t + 1))
            dve.wait_ge(pe_wo, 2 * t + 2)
            if t == 0:
                dve.wait_ge(l1_in, 32)
            banks = ps[:, 2 * (t % 2):2 * (t % 2) + 2, :].rearrange("p b n -> p (b n)")
            link(V.scalar_tensor_tensor(hb[:, :], hb[:, :], ALPHA, banks, ALU.mult, ALU.add))
            row_stats(t, hb[:, :]).then_inc(dve_r, 1)
            dve.wait_ge(pool_rstd, NT + 1 + t + 1)
            dve.wait_ge(dve_r, t + 1)
            norm(hb[:, :], mv[:, t % 2, 0:1], rstd[:, t % 2, 0:1], l1g[:, :], l1b[:, :]).then_inc(dve_h1, 1)
            dve.wait_ge(act_h1hi, t + 1)
            b0 = 4 + 2 * (t % 2)
            ts = slice(P * t, P * (t + 1))
            V.tensor_tensor(h1T_lo[:, :, ts], ps[:, b0:b0 + 2, :].rearrange("p b (k n) -> p (b k) n", n=P),
                            h1T_hi[:, :, ts].bitcast(F32), ALU.subtract).then_inc(dve_h1lo, 1)

        def u_low(b, u):
            f, H = divmod(u, 2)
            hs = slice(HALF * H, HALF * (H + 1))
            dve.wait_ge(act_uhi, 8 * b + u + 1)
            V.tensor_tensor(u_lo[:, f, hs], us[:, u % 2, :], u_hi[:, f, hs].bitcast(F32), ALU.subtract
                            ).then_inc(dve_ulo, 1)

        def y_out(t):
            dve.wait_ge(pool_rstd, NT + 1 + NT + t + 1)
            dve.wait_ge(dve_r, NT + t + 1)
            norm(y[:, t, :], mv[:, t % 2, 0:1], rstd[:, t % 2, 0:1], l2g[:, :], l2b[:, :]).then_inc(dve_out, 1)

        def ff_block(b, first, last):
            for u in range(2 * FT):
                dve.wait_ge(act_ur, 8 * b + u + 1)
                if not (first and u < 2):
                    dve.wait_ge(act_uhi, 8 * b + u - 1)
                    dve.wait_ge(dve_ulo, 8 * b + u - 1)
                V.scalar_tensor_tensor(us[:, u % 2, :], ps[:, u % 4, :], 0.0, ur[:, u % 2, :], ALU.max, ALU.mult
                                       ).then_inc(dve_us, 1)
                if u >= 1:
                    u_low(b, u - 1)
            u_low(b, 2 * FT - 1)
            if first:
                dve.wait_ge(y_in, 16)
            else:
                dve.wait_ge(dve_y, 16 * b)
            for t in range(NT):
                for c in range(2):
                    n = 2 * t + c
                    dve.wait_ge(pe_down, 16 * b + n + 1)
                    yy = y[:, t, HALF * c:HALF * (c + 1)]
                    V.scalar_tensor_tensor(yy, yy, yscale[:, bass.ds(b, 1)], ps[:, 4 + n % 4, :], ALU.mult, ALU.add
                                           ).then_inc(dve_y, 1)
                if last:
                    dve.wait_ge(dve_y, 16 * b + 2 * t + 2)
                    row_stats(t, y[:, t, :]).then_inc(dve_r, 1)
                    if t == 0:
                        dve.wait_ge(l2_in, 32)
                    else:
                        y_out(t - 1)
            if last:
                y_out(NT - 1)

        ff_block(0, True, False)
        with dve.Fori(1, NBLK - 1) as i:
            ff_block(i, False, False)
        ff_block(NBLK - 1, False, True)

    block_guard.__exit__(None, None, None)
    for g in names.values():
        g.__exit__(None, None, None)
    ps_guard.__exit__(None, None, None)


_INS = ["x", "meta_tokens", "ln_emb_g", "ln_emb_b", "w_in", "b_gate", "lb_logits", "a_norm_g", "sink", "w_proj_a",
        "w_proj_b", "w_o", "ln1_g", "ln1_b", "w_up", "w_down", "ln2_g", "ln2_b"]


def constants():
    ident = np.eye(P, dtype=np.float32)
    s = np.arange(P)[:, None]
    parts = []
    for h in LEVELS:
        t = np.arange(P)[None, :]
        t = t[:, (t[0] // h) % 2 == 1]
        parts.append((s // (2 * h) == t // (2 * h)) & (s // h % 2 == 0))
    parts.append(s == np.arange(P)[None, :])
    mask = np.concatenate(parts, 1).astype(np.float32)
    half = 8
    inv = np.power(np.float32(500000.0), -np.arange(half, dtype=np.float32) / np.float32(half))
    pos = np.zeros((P, NT + 1), np.float32)
    pos[:, :NT] = META + np.arange(T).reshape(NT, P).T
    pos[:META, NT] = np.arange(META)
    ang = pos[:, :, None].astype(np.float32) * inv[None, None, :].astype(np.float32)
    rope = np.stack([np.cos(ang), np.sin(ang)], 2).astype(np.float32)
    return {"c_ident": ident, "c_mask": mask, "c_rope": rope}


def kernel(**inputs):
    import concourse.bacc as bacc
    from concourse.bass_utils import run_bass_kernel_spmd

    nc = bacc.Bacc("TRN2", target_bir_lowering=False, num_devices=1)
    arrays = {n: np.ascontiguousarray(inputs[n]) for n in _INS}
    arrays.update(constants())
    args = {n: nc.dram_tensor(f"in_{n}", a.shape, mybir.dt.from_np(a.dtype), kind="ExternalInput").ap()
            for n, a in arrays.items()}
    out = nc.dram_tensor("out_0", (1, T, D), F32, kind="ExternalOutput").ap()
    build(nc, out=out, **args)
    result = run_bass_kernel_spmd(nc, [{f"in_{n}": a for n, a in arrays.items()}], core_ids=[0])
    return result.results[0]["out_0"]
```

```python
import numpy as np
import concourse.bass as bass
from concourse import mybir

P = 128
D = 1024
T = 1024
META = 16
CHUNK = 64
TA = T + META
NT = T // P
KT = D // P
HEADS = 4
QH = 8
FF = 4096
NBLK = 8
FT = FF // NBLK // P
HALF = 512
LN_EPS = 1e-5
RMS_EPS = 1e-6
ALPHA = 2.0 ** 0.25
SCALE = 64 ** -0.5
TINY = 1e-19
NEG = -1e30
LEVELS = [32, 16, 8, 4, 2, 1]
NL = len(LEVELS)
LVW = NL * CHUNK // 2
KD, QE = NL, NL + 1
SLOTS = 8
F_CUTS = [0, 348, 694, TA]
N_FU = 3 * HEADS
C_Q, C_F, C_I, C_G, C_BQ, C_BK, C_GATE = 0, 512, 1024, 1536, 2048, 2560, 2816

F32 = mybir.dt.float32
F32R = mybir.dt.float32r
ALU = mybir.AluOpType
ACT = mybir.ActivationFunctionType
AX = mybir.AxisListType.X

N_C = 22
N_D = N_C + 2 * NT
N_E = N_D + 8
N_F = N_E + 8
SLOT_GA, SLOT_GB = 6, 7
WO_UNITS = [(0, 0), (1, 0), (0, 1), (1, 1)] + [(t, c) for t in range(2, NT) for c in range(2)]


class Tally:

    def __init__(self, sem):
        self.sem, self.n, self.var, self.per = sem, 0, None, 0

    def now(self):
        return self.n if self.var is None else self.n + self.var * self.per

    def begin(self, var, per):
        self.var, self.per, self.start = var, per, self.n

    def end(self, times):
        assert self.n - self.start == self.per, (self.n - self.start, self.per)
        self.n = self.start + self.per * times
        self.var = None


def build(nc, x, meta_tokens, ln_emb_g, ln_emb_b, w_in, b_gate, lb_logits, a_norm_g, sink, w_proj_a,
          w_proj_b, w_o, ln1_g, ln1_b, w_up, w_down, ln2_g, ln2_b, c_ident, c_mask, c_rope, out):
    x = x.rearrange("b t d -> (b t) d")
    out = out.rearrange("b t d -> (b t) d")
    w_in = w_in.rearrange("l k n -> (l k) n")
    w_pa = w_proj_a.rearrange("l k n -> (l k) n")
    w_pb = w_proj_b.rearrange("l k n -> (l k) n")
    w_o = w_o.rearrange("l k n -> (l k) n")
    w_up = w_up.rearrange("l k n -> (l k) n")
    w_down = w_down.rearrange("l k n -> (l k) n")

    def internal(name, shape):
        return nc.dram_tensor(name, shape, F32, kind="Internal").ap()

    pair_d = internal("pair_scratch", [NT, P, 6, HALF])
    kT_d = internal("kT_scratch", [P, 2, CHUNK + T])
    vb_d = internal("vb_scratch", [CHUNK + T, P])
    gate_d = internal("gate_scratch", [2, KT, P, T])
    mix_d = internal("mix_scratch", [2, NT, P, HALF])
    h_d = internal("h_scratch", [NT, P, D])
    h1_d = internal("h1_scratch", [NT, P, D])

    base = [16512]
    limit = 229344

    def sb(name, shape, dt=F32, at=None):
        o = base[0] if at is None else at
        nbytes = 4 * int(np.prod(shape[1:]))
        t = nc.alloc_sbuf_tensor_at(name, shape, dt, offset=o)
        if at is None:
            base[0] = (o + nbytes + 31) // 32 * 32
        assert o + nbytes <= limit, (name, o + nbytes)
        return t

    R1 = base[0]
    hT_hi = sb("hT_hi", [P, KT, TA], F32R)
    hT_lo = sb("hT_lo", [P, KT, TA], F32R)
    mT_hi = sb("mT_hi", [P, KT, T], F32R, at=R1)
    mT_lo = sb("mT_lo", [P, KT, T], F32R, at=R1 + 4 * KT * T)
    u_hi = sb("u_hi", [P, FT, T], F32R, at=R1)
    u_lo = sb("u_lo", [P, FT, T], F32R, at=R1 + 4 * FT * T)
    y = sb("y", [P, NT, D], F32, at=R1 + 8 * FT * T)
    w_hi = sb("w_hi", [P, SLOTS, D], F32R)
    RL = base[0]
    w_lo = sb("w_lo", [P, SLOTS, D], F32R)
    w_raw = sb("w_raw", [P, SLOTS, D], F32, at=RL)
    ident = sb("ident", [P, P])
    lbl = sb("lbl", [P, 2, HEADS])
    lbe = sb("lbe", [P, 2, HEADS])
    lbm = sb("lbm", [P, HEADS])
    lb = sb("lb", [P, HEADS])
    oml = sb("oml", [P, HEADS])
    noml = sb("noml", [P, HEADS])
    normg = sb("normg", [P, HEADS])
    bgate = sb("bgate", [P, 2, KT])
    sinks = sb("sinks", [P, QH])
    negsink = sb("negsink", [P, QH])
    stats = sb("stats", [P, 2, 2, 6])
    mv = sb("mv", [P, 2, 2])
    rstd = sb("rstd", [P, 2, 2])
    neghalf = sb("neghalf", [P, 4])
    yscale = sb("yscale", [P, NBLK])
    R2 = base[0] = (base[0] + 31) // 32 * 32
    xb = sb("xb", [P, 3, D])
    lng = sb("lng", [P, D])
    lnb = sb("lnb", [P, D])
    fst = sb("fst", [P, HEADS, TA])
    st = sb("st", [P, 6, HALF])
    sg = sb("sg", [P, 2, HALF])
    qtm = sb("qtm", [P, 2, HALF])
    A_end = base[0]
    ktm = sb("ktm", [P, 4, 2, 2, 64], at=R2)
    kTs = sb("kTs", [P, 4, 2, P], at=R2 + 4096)
    vst = sb("vst", [P, 4, P], at=R2 + 8192)
    rope = sb("rope", [P, NT + 1, 2, 8], at=R2 + 10240)
    rtmp = sb("rtmp", [P, 4, QH * 8], at=R2 + 10240 + 576)
    scanmask = sb("scanmask", [P, TA], at=R2 + 12288)
    kmeta = sb("kmeta", [P, HEADS, META], at=R2 + 12288 + 4160)
    dmeta = sb("dmeta", [P, HEADS, META], at=R2 + 12288 + 4416)
    vmeta = sb("vmeta", [META, HALF])
    vmb = sb("vmb", [P, HALF])
    zero = sb("zero", [P, P])
    pin = sb("pin", [P, 3, HALF])
    S0 = sb("S0", [P, HEADS, P])
    kwin = sb("kwin", [P, 2, 2, META + P])
    vwin = sb("vwin", [P, 2, P])
    C_keep = base[0]
    base[0] = R2
    X = sb("X", [P, NL + 2, HALF])
    masks = sb("masks", [P, LVW + CHUNK])
    Amat = sb("Amat", [P, HEADS, CHUNK])
    prod = sb("prod", [P, HEADS, LVW])
    pv_ = sb("pv", [P, HALF])
    pqT = sb("pqT", [P, HEADS, P])
    kdT = sb("kdT", [P, HALF])
    C_mix = base[0] = R2 + 8 * 4 * HALF * 2
    pg = sb("pg", [P, HALF])
    prob = sb("prob", [P, QH, META + P])
    probT = sb("probT", [P, QH, P])
    probm = sb("probm", [P, P])
    probmT = sb("probmT", [P, P])
    S1 = sb("S1", [P, HEADS, P])
    o_sb = sb("o_sb", [P, HEADS, P])
    osq = sb("osq", [P, HEADS, P])
    ob = sb("ob", [P, QH, 64])
    gst = sb("gst", [P, 2, HALF])
    assert base[0] <= A_end, (base[0], A_end)
    base[0] = C_keep
    oast = sb("oast", [P, HALF])
    obst = sb("obst", [P, HALF])
    decay = sb("decay", [P, HEADS, 2])
    rowmax = sb("rowmax", [P, QH])
    negmax = sb("negmax", [P, QH])
    sinkexp = sb("sinkexp", [P, QH])
    rowsum = sb("rowsum", [P, QH])
    rden = sb("rden", [P, QH])
    osum = sb("osum", [P, HEADS])
    orms = sb("orms", [P, HEADS])
    base[0] = R2
    mix0_lo = sb("mix0_lo", [P, 2, 4, HALF], F32R)
    mix0_raw = sb("mix0_raw", [P, 2, 4, HALF], F32, at=R2)
    mix0_hi = sb("mix0_hi", [P, 2, 4, HALF], F32R)
    assert base[0] == C_mix
    mix1_hi = sb("mix1_hi", [P, 2, 4, HALF], F32R)
    RX1 = base[0]
    mix1_lo = sb("mix1_lo", [P, 2, 4, HALF], F32R)
    mix1_raw = sb("mix1_raw", [P, 2, 4, HALF], F32, at=RX1)
    mix_hi, mix_lo, mix_raw = (mix0_hi, mix1_hi), (mix0_lo, mix1_lo), (mix0_raw, mix1_raw)
    RE = base[0]
    gt = sb("gt", [P, 2, 2, HALF])
    t1 = sb("t1", [P, HALF])
    t2 = sb("t2", [P, HALF])
    base[0] = R2
    h1T_hi = sb("h1T_hi", [P, NT, KT, P], F32R)
    h1T_lo = sb("h1T_lo", [P, NT, KT, P], F32R)
    assert base[0] == RE
    hb0 = sb("hb0", [P, D])
    hb1 = sb("hb1", [P, D], at=RE - 4 * D)
    hb2 = sb("hb2", [P, D], at=RE - 4 * D - 4 * NT * D)
    hbs = (hb0, hb1, hb2)
    l1g = sb("l1g", [P, D])
    l1b = sb("l1b", [P, D])
    base[0] = RE
    ur = sb("ur", [P, 2, HALF])
    us = sb("us", [P, 2, HALF])
    l2g = sb("l2g", [P, D], at=RE)
    l2b = sb("l2b", [P, D], at=RE + 4096)

    ps_guard = nc.psum_tensor("ps", [P, 8, HALF], F32)
    ps = ps_guard.__enter__()

    names = {}

    def sem(name):
        names[name] = nc.semaphore(name)
        return names[name].__enter__()

    x_in = [sem(f"x_in{i}") for i in range(3)]
    tab_in = sem("tables_in")
    small_in = sem("small_tables_in")
    rope_in = sem("rope_in")
    h_saved = [sem(f"h_saved{i}") for i in range(3)]
    st_saved = [sem(f"stage_saved{i}") for i in range(6)]
    kv_saved = [sem(f"kv_saved{i}") for i in range(4)]
    pad_saved = sem("pads_saved")
    b_saved = sem("b_saved")
    vmb_in = sem("vmeta_blocks_in")
    w_landed = [sem(f"w_landed{i}") for i in range(SLOTS)]
    qkb_in, v_in, g_in, q_in, vw_in = sem("qkb_in"), sem("v_in"), sem("g_in"), sem("qT_in"), sem("vwin_in")
    mask_in = sem("masks_in")
    gate_saved = [sem(f"gate_saved{i}") for i in range(2)]
    oa_saved, ob_saved = sem("oa_saved"), sem("ob_saved")
    mix_in = [sem(f"mix_in{i}") for i in range(4)]
    gt_in = [sem(f"gt_in{i}") for i in range(2)]
    hb_in = [sem(f"hb_in{i}") for i in range(3)]
    h1_saved = [sem(f"h1_saved{i}") for i in range(3)]
    l1_in, y_in, l2_in, out_saved = sem("ln1_in"), sem("y_in"), sem("ln2_in"), sem("out_saved")
    w_split = sem("w_split")
    pool_const, pool_rstd, pool_D, pool_probm, pool_orms = (sem("pool_const"), sem("pool_rstd"), sem("pool_D"),
                                                            sem("pool_probm"), sem("pool_orms"))
    pool_seq = sem("pool_seq")
    pool_passed, act_passed, pe_passed = sem("pool_passed"), sem("act_passed"), sem("pe_passed")
    pe_hT, pe_tm, pe_cm, pe_qT, pe_kT, pe_meta = (sem("pe_hT"), sem("pe_tm"), sem("pe_cm"),
                                                         sem("pe_qT"), sem("pe_kT"), sem("pe_meta"))
    pe_lv, pe_kdT, pe_gate, pe_U, pe_sc, pe_o, pe_PT, pe_PV, pe_oT, pe_obT = (
        sem(n) for n in ("pe_levels", "pe_kdT", "pe_gate", "pe_U", "pe_scores", "pe_o", "pe_probT", "pe_PV", "pe_oT",
                         "pe_obT"))
    pe_mix, pe_wo, pe_h1T, pe_up, pe_down = (sem("pe_mix"), sem("pe_wo"), sem("pe_h1T"), sem("pe_up"), sem("pe_down"))
    act_whi, dve_wlo = sem("act_w_hi"), sem("dve_w_lo")
    act_lb, act_hi, act_tm, act_cm, act_qT, act_kT, act_ln, act_meta = (
        sem(n) for n in ("act_lb", "act_hT_hi", "act_tm", "act_cm", "act_qT", "act_kT", "act_ln",
                         "act_meta"))
    act_kdT, act_gate, act_prob, act_es, act_E, act_E7, act_dec, act_o, act_PT, act_ob = (
        sem(n) for n in ("act_kdT", "act_gate", "act_prob", "act_sinkexp", "act_E", "act_E_qe", "act_decay", "act_o",
                         "act_probT", "act_ob"))
    act_mixhi, act_sig, act_mhi, act_h1hi, act_ur, act_uhi = (sem(n) for n in (
        "act_mix_hi", "act_sig", "act_m_hi", "act_h1T_hi", "act_relu", "act_u_hi"))
    dve_seq = sem("dve_seq")
    dve_const, dve_lb, dve_stats, dve_h, dve_lo, dve_rope, dve_krope, dve_k, dve_f, dve_scan, dve_meta, dve_kdm, \
        dve_silu = (sem(n) for n in ("dve_const", "dve_lb", "dve_stats", "dve_h", "dve_hT_lo", "dve_rope",
                                     "dve_krope", "dve_k", "dve_f", "dve_scan", "dve_metasub", "dve_kdmeta",
                                     "dve_silu"))
    dve_prod, dve_A, dve_S, dve_nb, dve_osum, dve_X, dve_Xq, dve_on, dve_oa, dve_ob, dve_snk = (
        sem(n) for n in ("dve_prod", "dve_A", "dve_S", "dve_negmax", "dve_osum", "dve_X", "dve_X_qe", "dve_on",
                         "dve_oa", "dve_ob", "dve_sink"))
    dve_mixlo, dve_m, dve_mlo, dve_r, dve_h1, dve_h1lo, dve_us, dve_ulo, dve_y, dve_out = (
        sem(n) for n in ("dve_mix_lo", "dve_m", "dve_m_lo", "dve_r", "dve_h1", "dve_h1T_lo", "dve_usq",
                         "dve_u_lo", "dve_y", "dve_out"))

    def seen(eng, s, v):
        if not (isinstance(v, int) and v <= 0):
            eng.wait_ge(s, v)

    def passed(eng, s, v):
        if not isinstance(v, int):
            eng.sem_inc(s, 1)

    def kview(w, cols, k0=0, kn=KT):
        return w[k0 * P:(k0 + kn) * P, cols].rearrange("(k p) n -> p k n", p=P)

    def slot(t, s, k):
        return t[:, s, :].rearrange("p (k n) -> p k n", k=k)

    def as_pairs(t):
        return t.rearrange("p (q n) -> p q n", n=P)

    block_guard = nc.Block()
    block = block_guard.__enter__()

    def cols(c, n):
        return slice(c, c + n)

    a_granules = [kview(w_in, cols(C_I, HALF), 2 * g, 2) for g in range(4)]
    a_granules += [kview(w_in, cols(C_BQ, HALF), 2 * g, 2) for g in range(4)]
    a_granules += [kview(w_in, cols(C_BK, 256), 4 * g, 4) for g in range(2)]
    for c in (C_F, C_Q, C_G):
        a_granules += [kview(w_in, cols(c + P * j, P)) for j in range(4)]
    assert len(a_granules) == N_C

    def a_slot_free(n):
        m = n - SLOTS
        if m < 4:
            return pe_tm, 9
        if m < 8:
            return pe_tm, 17
        if m < 10:
            return pe_tm, 26
        return pe_cm, 3 * (m - 9)

    def st_free(eng, idx):
        seen(eng, st_saved[idx % 6], 16 * (idx // 6))

    def st_all_saved(eng, before):
        for i in range(6):
            eng.wait_ge(st_saved[i], 16 * len(range(i, before, 6)))

    def h1_all_saved(eng):
        for i in range(3):
            eng.wait_ge(h1_saved[i], 16 * len(range(i, NT, 3)))

    @block.sync
    def _(sp):
        def load_weights(src, s, k):
            return nc.sync.dma_start(slot(w_raw, s, k), src)

        def x_tile(t):
            if t >= 3:
                sp.wait_ge(pe_hT, t - 2)
                sp.wait_ge(h_saved[t % 3], 16 * (t // 3))
            if t < NT:
                sp.dma_start(xb[:, t % 3, :], x[P * t:P * (t + 1), :]).then_inc(x_in[t % 3], 16)
            else:
                sp.dma_start(xb[0:META, t % 3, :], meta_tokens).then_inc(x_in[t % 3], 16)

        x_tile(0)
        sp.dma_start(lng[:, :], ln_emb_g.partition_broadcast(P)).then_inc(tab_in, 16)
        sp.dma_start(lnb[:, :], ln_emb_b.partition_broadcast(P)).then_inc(tab_in, 16)
        sp.dma_start(ident[:, :], c_ident).then_inc(tab_in, 16)
        for n in range(2):
            load_weights(a_granules[n], n, 2).then_inc(w_landed[n], 16)
        x_tile(1)
        for n in range(2, 4):
            load_weights(a_granules[n], n, 2).then_inc(w_landed[n], 16)
        x_tile(2)
        with nc.allow_non_contiguous_dma(reason="small per-channel tables"):
            sp.dma_start(lbl[:, :, :], lb_logits.rearrange("a (h p) -> p a h", p=P)).then_inc(small_in, 16)
            sp.dma_start(normg[:, :], a_norm_g.rearrange("l (h p) -> p (l h)", p=P)).then_inc(small_in, 16)
            sp.dma_start(bgate[:, :, :], b_gate.rearrange("l (a k p) -> p (l a) k", a=2, p=P)).then_inc(small_in, 16)
        sp.dma_start(sinks[:, :], sink[0].partition_broadcast(P)).then_inc(small_in, 16)
        for n in range(4, SLOTS):
            x_tile(n - 1)
            load_weights(a_granules[n], n, 2).then_inc(w_landed[n], 16)
        sp.wait_ge(pool_const, 1)
        sp.dma_start(kT_d[:, :, 0:CHUNK], zero[:, :].rearrange("p (j n) -> p j n", j=2)).then_inc(pad_saved, 16)
        sp.dma_start(vb_d[0:CHUNK, :], zero[0:CHUNK, :]).then_inc(pad_saved, 16)
        for t in range(7, NT + 1):
            x_tile(t)
        sp.wait_ge(pe_hT, NT + 1)
        for i in range(3):
            sp.wait_ge(h_saved[i], (48, 48, 32)[i])
        sp.dma_start(rope[:, :, :, :], c_rope).then_inc(rope_in, 16)
        for n in range(SLOTS, N_C):
            sp.wait_ge(*a_slot_free(n))
            k = 2 if n < 8 else (4 if n < 10 else 8)
            load_weights(a_granules[n], n % SLOTS, k).then_inc(w_landed[n % SLOTS], 16)
            if n == 15:
                sp.wait_ge(act_tm, 26)
                sp.wait_ge(dve_const, 1)
                for h in range(QH):
                    j = h // 4
                    sp.dma_start(vmb[META * h:META * (h + 1), 64 * h:64 * (h + 1)],
                                 vst[0:META, 0, 64 * j:64 * (j + 1)]).then_inc(vmb_in, 16)

        def load_qkb(p):
            sp.dma_start(pin[:, :, :], pair_d[bass.ds(p, 1), :, 0:3, :].rearrange("a p s n -> p (a s) n")
                         ).then_inc(qkb_in, 16)

        def load_att(p):
            sp.dma_start(pqT[:, :, :].rearrange("p h n -> p (h n)"),
                         pair_d[bass.ds(p, 1), :, 5, :].rearrange("a p n -> p (a n)")).then_inc(q_in, 16)
            for c in range(2):
                sp.dma_start(kwin[:, :, c, META:META + P], kT_d[:, :, bass.ds(P * p + CHUNK * c, P)]
                             ).then_inc(q_in, 16)

        def load_v(p):
            sp.dma_start(pv_[:, :], pair_d[bass.ds(p, 1), :, 3, :].rearrange("a p n -> p (a n)")).then_inc(v_in, 16)

        def load_vwin(p):
            sp.dma_start(vwin[:, 0, :], vb_d[bass.ds(P * p, P), :]).then_inc(vw_in, 16)
            sp.dma_start(vwin[:, 1, :], vb_d[bass.ds(P * p + CHUNK, P), :]).then_inc(vw_in, 16)

        def load_g(p):
            sp.dma_start(pg[:, :], pair_d[bass.ds(p, 1), :, 4, :].rearrange("a p n -> p (a n)")).then_inc(g_in, 16)

        def load_gate(p, which):
            s = (SLOT_GA, SLOT_GB)[which]
            load_weights(w_in[:, bass.ds(C_GATE + D * which + P * p, P)].rearrange("(k p) n -> p k n", p=P), s, 8
                         ).then_inc(w_landed[s], 16)

        def load_proj(j):
            for a, w in enumerate((w_pa, w_pb)):
                sp.dma_start(slot(w_raw, j, 8)[:, 4 * a:4 * a + 4, :], kview(w, cols(P * j, P), 0, 4)
                             ).then_inc(w_landed[j], 16)

        sp.wait_ge(pe_cm, N_FU + 2)
        load_gate(0, 0)
        sp.wait_ge(pe_cm, N_FU + 4)
        load_gate(0, 1)
        sp.wait_ge(pe_cm, N_FU + 6)
        load_proj(0)
        sp.wait_ge(b_saved, 64)
        st_all_saved(sp, 32)
        load_qkb(0)
        for i in range(4):
            sp.wait_ge(kv_saved[i], 64)
        sp.wait_ge(pad_saved, 32)
        load_vwin(0)
        sp.wait_ge(dve_kdm, 1)
        sp.wait_ge(pe_meta, 1)
        load_v(0)
        load_att(0)
        sp.dma_start(masks[:, :], c_mask).then_inc(mask_in, 16)
        for j in range(1, 6):
            sp.wait_ge(pe_cm, N_FU + 6 + 2 * j)
            load_proj(j)
        st_all_saved(sp, 40)
        load_g(0)

        with sp.Fori(0, NT - 1) as i:
            sp.wait_ge(pe_lv, i + 1)
            sp.wait_ge(act_dec, i + 1)
            sp.wait_ge(act_E7, i + 1)
            sp.wait_ge(dve_Xq, i + 1)
            load_qkb(i + 1)
            sp.wait_ge(pe_sc, 2 * i + 2)
            load_att(i + 1)
            sp.wait_ge(pe_gate, 4 * i + 2)
            load_gate(i + 1, 0)
            sp.wait_ge(pe_o, i + 1)
            load_v(i + 1)
            sp.wait_ge(pe_PV, i + 1)
            load_vwin(i + 1)
            sp.wait_ge(pe_gate, 4 * i + 4)
            load_gate(i + 1, 1)
            sp.wait_ge(dve_oa, i + 1)
            load_g(i + 1)
        sp.wait_ge(pe_gate, 4 * NT - 2)
        load_proj(6)

        def load_mix(H):
            for a in range(2):
                sp.dma_start(mix_raw[H][:, a, :, :], mix_d[a, 4 * H:4 * H + 4].rearrange("q p n -> p q n")
                             ).then_inc(mix_in[2 * H + a], 16)

        def load_gates(n):
            H, j = divmod(n, KT)
            if n >= 2:
                sp.wait_ge(dve_m, n - 1)
            sp.dma_start(gt[:, n % 2, :, :],
                         gate_d[:, j, :, HALF * H:HALF * (H + 1)].rearrange("a p n -> p a n")
                         ).then_inc(gt_in[n % 2], 16)

        sp.wait_ge(pe_o, NT)
        sp.wait_ge(oa_saved, 16 * (NT - 1))
        sp.wait_ge(ob_saved, 16 * (NT - 1))
        load_mix(0)
        sp.wait_ge(pe_PV, NT)
        sp.wait_ge(gate_saved[0], 32 * NT - 32)
        load_gates(0)
        load_gates(1)
        sp.wait_ge(pe_gate, 4 * NT)
        load_proj(7)
        sp.wait_ge(oa_saved, 16 * NT)
        sp.wait_ge(ob_saved, 16 * NT)
        sp.wait_ge(pe_obT, NT)
        sp.wait_ge(act_ob, NT)
        sp.wait_ge(dve_oa, NT)
        for i in range(2):
            sp.wait_ge(gate_saved[i], 16 * 2 * NT)
        load_mix(1)
        for n in range(2, 2 * KT):
            load_gates(n)
            H, j = divmod(n, KT)
            if H == 1:
                sp.wait_ge(pe_mix, n + 1)
                c, g = divmod(j, 4)
                load_weights(kview(w_o, cols(HALF * c, HALF), 2 * g, 2), j, 2).then_inc(w_landed[j], 16)

        sp.wait_ge(dve_m, 16)
        sp.wait_ge(act_mhi, 16)
        sp.wait_ge(dve_mlo, 16)
        for t in range(2):
            sp.dma_start(hbs[t][:, :], h_d[t]).then_inc(hb_in[t], 16)
        sp.dma_start(l1g[:, :], ln1_g[0].partition_broadcast(P)).then_inc(l1_in, 16)
        sp.dma_start(l1b[:, :], ln1_b[0].partition_broadcast(P)).then_inc(l1_in, 16)
        for t in range(2, NT):
            if t >= 3:
                sp.wait_ge(pe_h1T, t - 2)
                sp.wait_ge(h1_saved[t % 3], 16 * (t // 3))
            sp.dma_start(hbs[t % 3][:, :], h_d[t]).then_inc(hb_in[t % 3], 16)

        def load_block(b, prior):
            for f in range(FT):
                if prior is None:
                    sp.wait_ge(pe_wo, 2 * NT - 1)
                else:
                    sp.wait_ge(pe_up, 8 * prior + FT + f + 1)
                load_weights(w_up[:, bass.ds(HALF * b + P * f, P)].rearrange("(k p) n -> p k n", p=P), f, 8
                             ).then_inc(w_landed[f], 16)
            for c in range(2):
                for g in range(2):
                    s = 4 + 2 * c + g
                    if prior is None:
                        sp.wait_ge(pe_wo, 2 * NT)
                    else:
                        sp.wait_ge(pe_down, 16 * prior + 15 + c)
                    load_weights(w_down[bass.ds(HALF * b + 2 * P * g, 2 * P), HALF * c:HALF * (c + 1)]
                                 .rearrange("(k p) n -> p k n", p=P), s, 2).then_inc(w_landed[s], 16)

        load_block(0, None)
        sp.wait_ge(pe_wo, 2 * NT)
        h1_all_saved(sp)
        sp.dma_start(y[:, :, :], h1_d.rearrange("t p n -> p t n")).then_inc(y_in, 16)
        with sp.Fori(0, NBLK - 1) as i:
            load_block(i + 1, i)
        sp.wait_ge(dve_ulo, 8 * NBLK)
        sp.wait_ge(act_uhi, 8 * NBLK)
        sp.dma_start(l2g[:, :], ln2_g[0].partition_broadcast(P)).then_inc(l2_in, 16)
        sp.dma_start(l2b[:, :], ln2_b[0].partition_broadcast(P)).then_inc(l2_in, 16)
        for t in range(NT):
            sp.wait_ge(dve_out, t + 1)
            sp.dma_start(out[P * t:P * (t + 1), :], y[:, t, :]).then_inc(out_saved, 16)
        sp.wait_ge(out_saved, 16 * NT)

    landed_before_D = [48] * 6 + [16 * (2 + NT)] * 2

    @block.gpsimd
    def _(pool):
        seq = Tally(pool_seq)

        def link(ins):
            ins.then_inc(pool_seq, 1)
            seq.n += 1
            pool.wait_ge(pool_seq, seq.now())

        def split(n, s, uses):
            pool.wait_ge(w_landed[s], uses)
            passed(pool, pool_passed, uses)
            nc.gpsimd.tensor_scalar(w_hi[:, s, :], w_raw[:, s, :], 1.0, 1.0, ALU.mult, ALU.mult).then_inc(w_split, 1)
            pool.wait_ge(w_split, 2 * n + 1)
            nc.gpsimd.tensor_tensor(w_lo[:, s, :], w_raw[:, s, :], w_hi[:, s, :].bitcast(F32), ALU.subtract
                                    ).then_inc(w_split, 1)

        def inv_sqrt(dst, src, eps, rows, scale=1.0):
            link(nc.gpsimd.tensor_scalar(dst, src, scale, eps, ALU.mult, ALU.add))
            return nc.gpsimd.tensor_tensor(dst, dst, neghalf[0:rows, 0:dst.shape[1]], ALU.pow)

        link(nc.gpsimd.memset(neghalf[:, :], -0.5))
        nc.gpsimd.memset(zero[:, :], 0.0).then_inc(pool_const, 1)
        def low_part(n):
            pool.wait_ge(act_whi, n + 1)
            nc.gpsimd.tensor_tensor(w_lo[:, n, :], w_raw[:, n, :], w_hi[:, n, :].bitcast(F32), ALU.subtract
                                    ).then_inc(w_split, 6 if n == 2 else 2)

        for t in range(NT + 1):
            rows = P if t < NT else META
            pool.wait_ge(dve_stats, t + 1)
            if t >= 2:
                pool.wait_ge(dve_h, t - 1)
            inv_sqrt(rstd[0:rows, t % 2, 0:1], mv[0:rows, t % 2, 1:2], LN_EPS, rows).then_inc(pool_rstd, 1)
            if t == 0:
                low_part(2)
            elif t == 1:
                low_part(3)
            elif t < 6:
                split(t + 2, t + 2, 16)
        for n in range(SLOTS, N_C):
            split(n, n % SLOTS, 16 * (n // SLOTS + 1))

        def decays(p, first):
            pool.wait_ge(qkb_in, 16 * (p + 1))
            if first:
                pool.wait_ge(dve_scan, 4)
                pool.wait_ge(pe_kT, NT + 1)
                pool.wait_ge(vmb_in, 16 * QH)
                for i in range(4):
                    pool.wait_ge(kv_saved[i], 64)
            else:
                pool.wait_ge(pe_lv, p)
                pool.wait_ge(pe_kdT, p)
            for n, h in enumerate(LEVELS):
                b = pin[:, 2, :].rearrange("p (q h) -> p q h", h=2 * h)
                d = X[:, n, :].rearrange("p (q h) -> p q h", h=2 * h)
                mid = b[:, :, h - 1:h].to_broadcast([P, HALF // (2 * h), h])
                nc.gpsimd.tensor_tensor(d[:, :, 0:h], mid, b[:, :, 0:h], ALU.subtract).then_inc(pool_D, 1)
                nc.gpsimd.tensor_tensor(d[:, :, h:2 * h], b[:, :, h:2 * h], mid, ALU.subtract).then_inc(pool_D, 1)
            b = pin[:, 2, :].rearrange("p (q h) -> p q h", h=CHUNK)
            nc.gpsimd.tensor_tensor(X[:, KD, :].rearrange("p (q h) -> p q h", h=CHUNK),
                                    b[:, :, CHUNK - 1:CHUNK].to_broadcast([P, 2 * HEADS, CHUNK]), b, ALU.subtract
                                    ).then_inc(pool_D, 1)

        def pair(p, last):
            if not last:
                decays(p + 1, False)
            pool.wait_ge(act_prob, 2 * p + 2)
            seen(pool, pe_PT, 3 * p)
            passed(pool, pool_passed, p)
            nc.gpsimd.tensor_scalar(probm[:, :].rearrange("p (h m) -> p h m", m=META), prob[:, :, 0:META], 1.0, 1.0,
                                    ALU.mult, ALU.mult).then_inc(pool_probm, 1)
            if not last:
                split(N_C + 2 * p + 2, SLOT_GA, 16 * (p + 4))
            pool.wait_ge(pool_const, 1)
            pool.wait_ge(dve_osum, p + 1)
            seen(pool, dve_on, p)
            passed(pool, pool_passed, p)
            inv_sqrt(orms[:, :], osum[:, :], RMS_EPS, P, 1.0 / P).then_inc(pool_orms, 1)
            if not last:
                split(N_C + 2 * p + 3, SLOT_GB, 16 * (p + 4))

        split(N_C, SLOT_GA, 48)
        split(N_C + 1, SLOT_GB, 48)
        decays(0, True)
        pair(0, False)
        seq.begin(None, 0)
        with pool.Fori(0, NT - 2) as i:
            seq.begin(i, 1)
            pair(i + 1, False)
        seq.end(NT - 2)
        pair(NT - 1, True)
        for j in range(8):
            split(N_D + j, j, landed_before_D[j] + 32)
        for j in range(8):
            split(N_E + j, j, landed_before_D[j] + 48)
        def block_split(b, s0=0):
            for s in range(s0, 8):
                split(N_F + 8 * b + s, s, landed_before_D[s] + 64 + 16 * b)

        for t in range(NT):
            if t == NT - 1:
                for s in range(2):
                    split(N_F + s, s, landed_before_D[s] + 64)
            pool.wait_ge(dve_r, t + 1)
            inv_sqrt(rstd[:, t % 2, 0:1], mv[:, t % 2, 1:2], LN_EPS, P).then_inc(pool_rstd, 1)
        block_split(0, 2)
        with pool.Fori(0, NBLK - 1) as i:
            block_split(i + 1)
        for t in range(NT):
            pool.wait_ge(dve_r, NT + t + 1)
            inv_sqrt(rstd[:, t % 2, 0:1], mv[:, t % 2, 1:2], LN_EPS, P).then_inc(pool_rstd, 1)

    @block.tensor
    def _(pe):
        def mm(o, lhsT, rhs, start, stop):
            return nc.tensor.matmul(o, lhsT, rhs, start=start, stop=stop, skip_group_check=True)

        def gemm_w_stationary(o, s, k_of, moving_hi, moving_lo, ks, first=True, last=True):
            ins = None
            for n, k in enumerate(ks):
                a, z = first and n == 0, last and n == len(ks) - 1
                wh, wl = slot(w_hi, s, k_of)[:, k, :], slot(w_lo, s, k_of)[:, k, :]
                mm(o, wh, moving_hi(k), a, False)
                mm(o, wh, moving_lo(k), False, False)
                ins = mm(o, wl, moving_hi(k), False, z)
            return ins

        def gemm_w_moving(o, s0, per, still_hi, still_lo, nk, as_split=False, midway=None):
            ins = None
            for k in range(nk):
                s, kk = s0 + k // per, k % per
                if midway and k == nk - 4:
                    midway()
                if as_split and kk == 0:
                    if s < 2:
                        pe.wait_ge(dve_wlo, s + 1)
                    else:
                        pe.wait_ge(w_split, 2 * (s + 1))
                wh, wl = slot(w_hi, s, per)[:, kk, :], slot(w_lo, s, per)[:, kk, :]
                mm(o, still_hi(k), wh, k == 0, False)
                mm(o, still_hi(k), wl, False, False)
                ins = mm(o, still_lo(k), wh, False, k == nk - 1)
            return ins

        pe.wait_ge(tab_in, 48)

        def transpose_h(t):
            rows = P if t < NT else META
            pe.wait_ge(dve_h, t + 1)
            if t >= 2:
                pe.wait_ge(act_hi, t - 1)
                pe.wait_ge(dve_lo, t - 1)
            b0 = 4 + 2 * (t % 2)
            for k in range(KT):
                last = nc.tensor.transpose(ps[:, b0 + k // 4, P * (k % 4):P * (k % 4) + rows],
                                           xb[0:rows, t % 3, P * k:P * (k + 1)], ident[0:rows, 0:rows])
            last.then_inc(pe_hT, 1)

        def h_part(part, t):
            rows = P if t < NT else META
            return lambda k: part[:, k, P * t:P * t + rows]

        def token_unit(u, t, s0, per, n, width, midway=None):
            rows = P if t < NT else META
            if u >= 2:
                pe.wait_ge(act_tm, u - 1)
            if u > 0:
                pe.wait_ge(w_split, 2 * n)
            o = ps[0:rows, u % 2, 0:width]
            ins = gemm_w_moving(o, s0, per, h_part(hT_hi, t), h_part(hT_lo, t), KT, as_split=u == 0,
                                midway=midway)
            ins.then_inc(pe_tm, 1)

        transpose_h(0)
        for t in range(NT + 1):
            pe.wait_ge(act_hi, t + 1)
            pe.wait_ge(dve_lo, t + 1)
            token_unit(t, t, 0, 2, 4, HALF, midway=(lambda: transpose_h(t + 1)) if t < NT else None)

        def transpose_q(t):
            pe.wait_ge(dve_rope, t + 1)
            if t >= 2:
                pe.wait_ge(act_qT, t - 1)
            for h in range(HEADS):
                last = nc.tensor.transpose(ps[:, 4 + t % 2, P * h:P * (h + 1)], qtm[:, t % 2, P * h:P * (h + 1)],
                                           ident[:, :])
            last.then_inc(pe_qT, 1)

        for t in range(NT):
            token_unit(9 + t, t, 4, 2, 8, HALF)
            if t >= 1:
                transpose_q(t - 1)

        def transpose_k(t):
            rows = P if t < NT else META
            pe.wait_ge(dve_krope, t + 1)
            if t >= 2:
                pe.wait_ge(act_kT, t - 1)
            for j in range(2):
                last = nc.tensor.transpose(ps[:, 6 + t % 2, P * j:P * j + rows],
                                           ktm[0:rows, t % 4, j, :, :].rearrange("p a b -> p (a b)"),
                                           ident[0:rows, 0:rows])
            last.then_inc(pe_kT, 1)

        for t in range(NT + 1):
            token_unit(17 + t, t, 0, 4, 10, 256)
            if t == 0:
                transpose_q(NT - 1)
            elif t >= 2:
                transpose_k(t - 2)

        def channel_unit(u, n, lo, hi):
            pe.wait_ge(w_split, 2 * (n + 1))
            ins = gemm_w_stationary(ps[:, u % 4, 0:hi - lo], n % SLOTS, 8, lambda k: hT_hi[:, k, lo:hi],
                                    lambda k: hT_lo[:, k, lo:hi], range(KT))
            ins.then_inc(pe_cm, 1)

        for u in range(N_FU):
            if u < 2:
                pe.wait_ge(act_tm, 25 + u)
            elif u >= 4:
                pe.wait_ge(act_cm, u - 3)
            channel_unit(u, 10 + u // 3, F_CUTS[u % 3], F_CUTS[u % 3 + 1])
            if u < 2:
                transpose_k(NT - 1 + u)
        for v in range(8, 24):
            u = N_FU - 8 + v
            if v < 12:
                pe.wait_ge(act_cm, u - 3)
            else:
                pe.wait_ge(dve_silu, v - 11)
            channel_unit(u, 10 + v // 2, HALF * (v % 2), HALF * (v % 2 + 1))
            if v == 15:
                pe.wait_ge(dve_kdm, 1)
                pe.wait_ge(act_kT, NT + 1)
                for hd in range(HEADS):
                    last = nc.tensor.transpose(ps[0:META, 6, P * hd:P * (hd + 1)], dmeta[:, hd, :], ident[:, :])
                last.then_inc(pe_meta, 1)
            if v == 17:
                pe.wait_ge(act_meta, 2)
                for hd in range(HEADS):
                    last = mm(ps[:, 7, P * hd:P * (hd + 1)], qtm[0:META, 0, P * hd:P * (hd + 1)],
                              vmeta[:, P * hd:P * (hd + 1)], True, True)
                last.then_inc(pe_meta, 1)

        def gate_unit(p, u, ks, first, last):
            a, H = divmod(u, 2)
            s = (SLOT_GA, SLOT_GB)[a]
            if first:
                pe.wait_ge(w_split, 2 * (N_C + 1 + 2 * p + a))
                if isinstance(p, int) and p == 0 and u < 2:
                    pe.wait_ge(dve_silu, 13 + u)
                else:
                    pe.wait_ge(act_gate, 4 * p + u - 1)
            ins = gemm_w_stationary(ps[:, H, :], s, 8, lambda k: hT_hi[:, k, HALF * H:HALF * (H + 1)],
                                    lambda k: hT_lo[:, k, HALF * H:HALF * (H + 1)], ks, first, last)
            if last:
                ins.then_inc(pe_gate, 1)

        def pair(p, first):
            one = p + 1
            pe.wait_ge(dve_X, one)
            if first:
                pe.wait_ge(act_meta, 3)
                pe.wait_ge(act_kT, NT + 1)
            else:
                pe.wait_ge(act_PT, 3 * p)
                pe.wait_ge(act_prob, 2 * p)
            for hd in range(HEADS):
                for n, h in enumerate(LEVELS + [0]):
                    for c in range(2):
                        cs = slice(P * hd + CHUNK * c, P * hd + CHUNK * (c + 1))
                        o = ps[CHUNK * c:CHUNK * (c + 1), 4 + hd // 2, 256 * (hd % 2) + CHUNK // 2 * n:]
                        if h:
                            right = X[:, n, cs].rearrange("p (q h) -> p q h", h=2 * h)[:, :, h:2 * h]
                            mm(o[:, 0:CHUNK // 2], X[:, n, cs], right, True, True)
                        else:
                            last = mm(o[:, 0:CHUNK], pin[:, 1, cs], pin[:, 0, cs], True, True)
            last.then_inc(pe_lv, 1)
            if not first:
                pe.wait_ge(act_ob, p)
            for hd in range(HEADS):
                last = nc.tensor.transpose(ps[:, 6, P * hd:P * (hd + 1)], X[:, KD, P * hd:P * (hd + 1)], ident[:, :])
            last.then_inc(pe_kdT, 1)
            gate_unit(p, 0, range(KT), True, True)
            pe.wait_ge(act_kdT, one)
            pe.wait_ge(v_in, 16 * one)
            if not first:
                pe.wait_ge(dve_oa, p)
            for hd in range(HEADS):
                for c in range(2):
                    rs, cs = slice(CHUNK * c, CHUNK * (c + 1)), slice(P * hd, P * (hd + 1))
                    last = mm(ps[:, 7 - c, cs], kdT[rs, cs], pv_[rs, cs], True, True)
                    if hd == HEADS - 1:
                        last.then_inc(pe_U, 1)
            pe.wait_ge(q_in, 48 * one)
            for g in range(2):
                if g == 1:
                    pe.wait_ge(dve_prod, one)
                passed(pe, pe_passed, p)
                for hh in range(4):
                    h = 4 * g + hh
                    j, ds = h // 4, slice(64 * (h % 2), 64 * (h % 2) + 64)
                    bank, off = 2 + 2 * g + hh % 2, 256 * (hh // 2)
                    for c in range(2):
                        o = ps[CHUNK * c:CHUNK * (c + 1), bank, off:off + META + P]
                        last = mm(o, pqT[ds, h // 2, CHUNK * c:CHUNK * (c + 1)], kwin[ds, j, c, :], True, True)
                last.then_inc(pe_sc, 1)
            gate_unit(p, 1, range(KT), True, True)
            pe.wait_ge(dve_A, one)
            pe.wait_ge(dve_S, 2 * p + 1)
            pe.wait_ge(dve_Xq, one)
            for hd in range(HEADS):
                cs = slice(P * hd, P * (hd + 1))
                for c in range(2):
                    rs = slice(CHUNK * c, CHUNK * (c + 1))
                    mm(ps[rs, 7, cs], X[:, QE, P * hd + CHUNK * c:P * hd + CHUNK * (c + 1)],
                       (S0, S1)[c][:, hd, :], True, False)
                    last = mm(ps[rs, 7, cs], Amat[rs, hd, :], pv_[rs, cs], False, True)
            last.then_inc(pe_o, 1)
            gate_unit(p, 2, range(KT), True, True)
            for g in range(2):
                pe.wait_ge(act_prob, 2 * p + g + 1)
                for hh in range(4):
                    last = nc.tensor.transpose(ps[:, 2 + 2 * g, P * hh:P * (hh + 1)],
                                               prob[:, 4 * g + hh, META:META + P], ident[:, :])
                last.then_inc(pe_PT, 1)
            pe.wait_ge(pool_probm, one)
            nc.tensor.transpose(ps[:, 3, 0:P], probm[:, :], ident[:, :]).then_inc(pe_PT, 1)
            gate_unit(p, 3, range(4), True, False)
            pe.wait_ge(act_PT, 3 * p + 3)
            pe.wait_ge(vw_in, 32 * one)
            pe.wait_ge(dve_S, 2 * p + 2)
            if first:
                pe.wait_ge(vmb_in, 16 * QH)
            mm(ps[:, 6, :], probmT[:, :], vmb[:, :], True, False)
            for h in range(QH):
                for c in range(2):
                    last = mm(ps[CHUNK * c:CHUNK * (c + 1), 6, 64 * h:64 * (h + 1)],
                              probT[:, h, CHUNK * c:CHUNK * (c + 1)], vwin[:, c, 64 * (h // 4):64 * (h // 4) + 64],
                              False, True)
            last.then_inc(pe_PV, 1)
            gate_unit(p, 3, range(4, KT), False, True)
            pe.wait_ge(dve_on, one)
            for hd in range(HEADS):
                last = nc.tensor.transpose(ps[:, 7, P * hd:P * (hd + 1)], o_sb[:, hd, :], ident[:, :])
            last.then_inc(pe_oT, 1)
            pe.wait_ge(dve_ob, one)
            for hd in range(HEADS):
                last = nc.tensor.transpose(ps[:, 6, P * hd:P * (hd + 1)],
                                           ob[:, 2 * hd:2 * hd + 2, :].rearrange("p a b -> p (a b)"), ident[:, :])
            last.then_inc(pe_obT, 1)

        pair(0, True)
        with pe.Fori(1, NT) as i:
            pair(i, False)

        for n in range(2 * KT):
            H, j = divmod(n, KT)
            if H == 0:
                pe.wait_ge(w_split, 2 * (N_D + j + 1))
            if n == 0:
                pe.wait_ge(act_gate, 4 * NT)
            elif n == 1:
                pe.wait_ge(act_PT, 3 * NT)
            elif n == 3:
                pe.wait_ge(act_ob, NT)
                pe.wait_ge(dve_oa, NT)
            elif n >= 4:
                pe.wait_ge(dve_m, n - 3)
            for a in range(2):
                if j == 0:
                    pe.wait_ge(act_mixhi, 2 * H + a + 1)
                    pe.wait_ge(dve_mixlo, 2 * H + a + 1)
                ins = gemm_w_stationary(ps[:, 2 * (n % 4) + a, :], j, 8,
                                        lambda k: mix_hi[H][:, a, :, P * (k % 4):P * (k % 4) + P],
                                        lambda k: mix_lo[H][:, a, :, P * (k % 4):P * (k % 4) + P],
                                        range(4 * a, 4 * a + 4))
            ins.then_inc(pe_mix, 1)

        def transpose_h1(t):
            pe.wait_ge(dve_h1, t + 1)
            if t >= 2:
                pe.wait_ge(act_h1hi, t - 1)
                pe.wait_ge(dve_h1lo, t - 1)
            b0 = 4 + 2 * (t % 2)
            for k in range(KT):
                last = nc.tensor.transpose(ps[:, b0 + k // 4, P * (k % 4):P * (k % 4 + 1)],
                                           hbs[t % 3][:, P * k:P * (k + 1)], ident[:, :])
            last.then_inc(pe_h1T, 1)

        for u, (t, c) in enumerate(WO_UNITS):
            if t % 4 == 0 and c == 0:
                pe.wait_ge(act_mhi, 8 * (t // 4 + 1))
                pe.wait_ge(dve_mlo, 8 * (t // 4 + 1))
                pe.wait_ge(dve_m, 14)
            if t >= 2 and c == 0:
                pe.wait_ge(dve_r, t - 1)
            pe.wait_ge(w_split, 2 * (N_E + 4 * c + 4))
            ins = gemm_w_moving(ps[:, 2 * (t % 2) + c, :], 4 * c, 2, lambda k: mT_hi[:, k, P * t:P * (t + 1)],
                                lambda k: mT_lo[:, k, P * t:P * (t + 1)], KT)
            ins.then_inc(pe_wo, 1)
            if t >= 1 and c == 1:
                transpose_h1(t - 1)

        def ff_block(b, first):
            for u in range(2 * FT):
                H, f = divmod(u, FT)
                if first:
                    if u == 0:
                        pe.wait_ge(act_h1hi, 4)
                        pe.wait_ge(dve_h1lo, 4)
                        pe.wait_ge(dve_r, NT - 1)
                    if u == 2:
                        transpose_h1(NT - 1)
                        pe.wait_ge(dve_r, NT)
                    if u == FT:
                        pe.wait_ge(act_h1hi, NT)
                        pe.wait_ge(dve_h1lo, NT)
                if u >= 4 or not first:
                    pe.wait_ge(dve_us, 8 * b + u - 3)
                if H == 0:
                    pe.wait_ge(w_split, 2 * (N_F + 8 * b + f + 1))
                ins = gemm_w_stationary(ps[:, u % 4, :], f, 8, lambda k: h1T_hi[:, 4 * H:4 * H + 4, k, :],
                                        lambda k: h1T_lo[:, 4 * H:4 * H + 4, k, :], range(KT))
                ins.then_inc(pe_up, 1)
            for t in range(NT):
                if t % 4 == 0:
                    pe.wait_ge(act_uhi, 8 * b + t + 4)
                    pe.wait_ge(dve_ulo, 8 * b + t + 4)
                for c in range(2):
                    n = 2 * t + c
                    if not first or n >= 4:
                        pe.wait_ge(dve_y, 16 * b + n - 3)
                    if t == 0:
                        pe.wait_ge(w_split, 2 * (N_F + 8 * b + 6 + 2 * c))
                    ins = gemm_w_moving(ps[:, 4 + n % 4, :], 4 + 2 * c, 2, lambda k: u_hi[:, k, P * t:P * (t + 1)],
                                        lambda k: u_lo[:, k, P * t:P * (t + 1)], FT)
                    ins.then_inc(pe_down, 1)

        ff_block(0, True)
        with pe.Fori(1, NBLK) as i:
            ff_block(i, False)

    @block.scalar
    def _(act):
        fn = nc.scalar.activation

        def copy(dst, src):
            return fn(dst, src, ACT.Copy)

        def pair_view(idx, t):
            return pair_d[t, :, idx, :]

        def head_tokens(idx, hd, H):
            return pair_d[4 * H:4 * H + 4, :, idx, P * hd:P * (hd + 1)].rearrange("q p n -> p q n")


        def hT_high(t):
            n = P if t < NT else META
            act.wait_ge(pe_hT, t + 1)
            b0 = 4 + 2 * (t % 2)
            src = ps[:, b0:b0 + 2, :].rearrange("p b (k n) -> p (b k) n", n=P)[:, :, 0:n]
            copy(hT_hi[:, :, P * t:P * t + n], src).then_inc(act_hi, 1)

        def save_h(t):
            act.wait_ge(dve_h, t + 1)
            act.dma_start(h_d[t], xb[:, t % 3, :]).then_inc(h_saved[t % 3], 16)

        def save_st(idx, dst, made, count):
            act.wait_ge(made, count)
            act.dma_start(dst, st[:, idx % 6, :] if len(dst.shape) == 2 else as_pairs(st[:, idx % 6, :])
                          ).then_inc(st_saved[idx % 6], 16)

        def w_high(n):
            act.wait_ge(w_landed[n], 16)
            copy(w_hi[:, n, :], w_raw[:, n, :]).then_inc(act_whi, 1)

        w_high(0)
        w_high(1)
        save_h(0)
        hT_high(0)
        w_high(2)
        w_high(3)
        for t in range(NT + 1):
            if t < NT:
                if t + 1 < NT:
                    save_h(t + 1)
                hT_high(t + 1)
            act.wait_ge(pe_tm, t + 1)
            if t < NT:
                st_free(act, t)
                copy(st[:, t % 6, :], ps[:, t % 2, :]).then_inc(act_tm, 1)
            else:
                copy(vmeta[:, :], ps[0:META, t % 2, :]).then_inc(act_tm, 1)
            if t >= 1:
                save_st(t - 1, pair_view(3, t - 1), act_tm, t)
            if t == 2:
                act.wait_ge(dve_lb, 1)
                fn(lbe[:, :, :], lbl[:, :, :], ACT.Exp).then_inc(act_lb, 1)

        def qT_out(t):
            act.wait_ge(pe_qT, t + 1)
            st_free(act, 8 + t)
            copy(st[:, (8 + t) % 6, :], ps[:, 4 + t % 2, :]).then_inc(act_qT, 1)

        for t in range(NT):
            act.wait_ge(pe_tm, 10 + t)
            if t >= 2:
                act.wait_ge(pe_qT, t - 1)
            copy(qtm[:, t % 2, :], ps[:, (9 + t) % 2, :]).then_inc(act_tm, 1)
            if t >= 1:
                qT_out(t - 1)
            if t >= 2:
                save_st(8 + t - 2, pair_view(5, t - 2), act_qT, t - 1)

        def kT_out(t):
            act.wait_ge(pe_kT, t + 1)
            src = ps[:, 6 + t % 2, 0:2 * P].rearrange("p (j n) -> p j n", j=2)
            if t < NT:
                copy(kTs[:, t % 4, :, :], src).then_inc(act_kT, 1)
            else:
                copy(kwin[:, :, 0, 0:META], src[:, :, 0:META])
                copy(kwin[:, :, 1, 0:META], src[:, :, 0:META]).then_inc(act_kT, 1)

        def save_kv(t):
            act.wait_ge(act_kT, t + 1)
            c0 = CHUNK + P * t
            act.dma_start(kT_d[:, :, c0:c0 + P], kTs[:, t % 4, :, :]).then_inc(kv_saved[t % 4], 16)
            act.dma_start(vb_d[c0:c0 + P, :], vst[:, t % 4, :]).then_inc(kv_saved[t % 4], 16)

        for i in range(3):
            act.wait_ge(h_saved[i], (48, 48, 32)[i])
        for t in range(NT + 1):
            rows = P if t < NT else META
            act.wait_ge(pe_tm, 18 + t)
            if t >= 4:
                act.wait_ge(pe_kT, t - 3)
                act.wait_ge(kv_saved[t % 4], 32 * (t // 4))
            src = ps[0:rows, (17 + t) % 2, :]
            copy(ktm[0:rows, t % 4, :, 0, :], src[:, 0:P].rearrange("p (j d) -> p j d", j=2))
            copy(vst[0:rows, t % 4, :], src[:, P:2 * P]).then_inc(act_tm, 1)
            if t == 0:
                qT_out(NT - 1)
                save_st(8 + NT - 2, pair_view(5, NT - 2), act_qT, NT - 1)
            elif t == 1:
                save_st(8 + NT - 1, pair_view(5, NT - 1), act_qT, NT)
            else:
                kT_out(t - 2)
                save_kv(t - 2)

        for u in range(N_FU):
            hd, i = divmod(u, 3)
            act.wait_ge(pe_cm, u + 1)
            fn(fst[:, hd, F_CUTS[i]:F_CUTS[i + 1]], ps[:, u % 4, 0:F_CUTS[i + 1] - F_CUTS[i]], ACT.Sigmoid
               ).then_inc(act_cm, 1)
            if u < 2:
                kT_out(NT - 1 + u)
            if u == 0:
                save_kv(NT - 1)
            if i == 2:
                for H in range(2):
                    v = 2 * hd + H
                    save_st(16 + v, head_tokens(1, hd, H), dve_k, v + 1)
        for hd in range(HEADS):
            act.wait_ge(dve_f, hd + 1)
            fn(fst[:, hd, :], fst[:, hd, :], ACT.Ln).then_inc(act_ln, 1)

        def silu_sigmoid(v):
            act.wait_ge(pe_cm, N_FU - 8 + v + 1)
            seen(act, dve_silu, v - 9)
            fn(sg[:, v % 2, :], ps[:, v % 4, :], ACT.Sigmoid).then_inc(act_cm, 1)
            if v >= 9:
                w = v - 1
                save_st(16 + w, head_tokens(0 if w < 16 else 4, w // 2 % 4, w % 2), dve_silu, w - 7)

        def exp_decays(p):
            act.wait_ge(pool_D, 13 * (p + 1))
            fn(X[:, 0:NL + 1, :], X[:, 0:NL + 1, :], ACT.Exp).then_inc(act_E, 1)

        def exp_qe(p):
            act.wait_ge(qkb_in, 16 * (p + 1))
            seen(act, pe_o, p)
            fn(X[:, QE, :], pin[:, 2, :], ACT.Exp).then_inc(act_E7, 1)

        def chunk_decay(p):
            seen(act, dve_S, 2 * p)
            b = pin[:, 2, :].rearrange("p (h c n) -> p h c n", h=HEADS, c=2)
            fn(decay[:, :, :], b[:, :, :, CHUNK - 1], ACT.Exp).then_inc(act_dec, 1)

        for v in range(8, 24):
            silu_sigmoid(v)
            if v == 9:
                for hd in range(HEADS):
                    act.wait_ge(dve_scan, hd + 1)
                    act.dma_start(pair_d[:, :, 2, P * hd:P * (hd + 1)].rearrange("q p n -> p q n"),
                                  as_pairs(fst[:, hd, 0:T])).then_inc(b_saved, 16)
            if v == 12:
                act.wait_ge(dve_meta, 1)
                fn(dmeta[:, :, :], dmeta[:, :, :], ACT.Exp).then_inc(act_meta, 1)
            if v == 16:
                act.wait_ge(pe_meta, 1)
                copy(qtm[0:META, 0, :], ps[0:META, 6, :]).then_inc(act_meta, 1)
            if v == 18:
                act.wait_ge(pe_meta, 2)
                copy(S0[:, :, :].rearrange("p h n -> p (h n)"), ps[:, 7, :]).then_inc(act_meta, 1)
            if v == 20:
                exp_decays(0)
                exp_qe(0)
                chunk_decay(0)
        save_st(39, head_tokens(4, 3, 1), dve_silu, 16)

        def gate_out(p, u):
            a, H = divmod(u, 2)
            act.wait_ge(pe_gate, 4 * p + u + 1)
            seen(act, gate_saved[H], 32 * p + 16 * a)
            act.wait_ge(small_in, 64)
            passed(act, act_passed, p)
            fn(gst[:, H, :], ps[:, H, :], ACT.Identity, bias=bgate[:, a, bass.ds(p, 1)]).then_inc(act_gate, 1)

        def save_gate(p, u):
            a, H = divmod(u, 2)
            act.wait_ge(act_gate, 4 * p + u + 1)
            act.dma_start(gate_d[a, bass.ds(p, 1), :, HALF * H:HALF * (H + 1)].rearrange("a p n -> p (a n)"),
                          gst[:, H, :]).then_inc(gate_saved[H], 16)

        def mix_high(H, a):
            act.wait_ge(mix_in[2 * H + a], 16)
            copy(mix_hi[H][:, a, :, :], mix_raw[H][:, a, :, :]).then_inc(act_mixhi, 1)

        def pair(p, first, last):
            one = p + 1
            act.wait_ge(pe_kdT, one)
            copy(kdT[:, :], ps[:, 6, :]).then_inc(act_kdT, 1)
            gate_out(p, 0)
            for g in range(2):
                act.wait_ge(dve_nb, 2 * p + g + 1)
                if not first:
                    act.wait_ge(pool_probm, p)
                    act.wait_ge(dve_ob, p)
                for hh in range(4):
                    h = 4 * g + hh
                    bank, off = 2 + 2 * g + hh % 2, 256 * (hh // 2)
                    ins = fn(prob[:, h, :], ps[:, bank, off:off + META + P], ACT.Exp, bias=negmax[:, h:h + 1],
                             scale=SCALE, accum_out=rowsum[:, h:h + 1])
                ins.then_inc(act_prob, 1)
            save_gate(p, 0)
            act.wait_ge(dve_snk, one)
            fn(sinkexp[:, :], sinkexp[:, :], ACT.Exp).then_inc(act_es, 1)
            if not last:
                exp_decays(p + 1)
            gate_out(p, 1)
            act.wait_ge(pe_o, one)
            copy(o_sb[:, :, :].rearrange("p h n -> p (h n)"), ps[:, 7, :]).then_inc(act_o, 1)
            save_gate(p, 1)
            if not last:
                exp_qe(p + 1)
            gate_out(p, 2)
            if not last:
                chunk_decay(p + 1)
            for g in range(2):
                act.wait_ge(pe_PT, 3 * p + g + 1)
                copy(probT[:, 4 * g:4 * g + 4, :].rearrange("p h n -> p (h n)"), ps[:, 2 + 2 * g, :]
                     ).then_inc(act_PT, 1)
            act.wait_ge(pe_PT, 3 * p + 3)
            copy(probmT[:, :], ps[:, 3, 0:P]).then_inc(act_PT, 1)
            save_gate(p, 2)
            if last:
                mix_high(0, 0)
                mix_high(0, 1)
            gate_out(p, 3)
            act.wait_ge(dve_oa, one)
            act.dma_start(mix_d[0, bass.ds(p, 1)].rearrange("a p n -> p (a n)"), oast[:, :]).then_inc(oa_saved, 16)
            act.wait_ge(pe_obT, one)
            seen(act, ob_saved, 16 * p)
            copy(obst[:, :], ps[:, 6, :]).then_inc(act_ob, 1)
            save_gate(p, 3)
            act.wait_ge(act_ob, one)
            act.dma_start(mix_d[1, bass.ds(p, 1)].rearrange("a p n -> p (a n)"), obst[:, :]).then_inc(ob_saved, 16)

        pair(0, True, False)
        with act.Fori(1, NT - 1) as i:
            pair(i, False, False)
        pair(NT - 1, False, True)

        def m_high(n):
            H, j = divmod(n, KT)
            act.wait_ge(dve_m, n + 1)
            copy(mT_hi[:, j, HALF * H:HALF * (H + 1)], t1[:, :]).then_inc(act_mhi, 1)

        for n in range(16):
            act.wait_ge(gt_in[n % 2], 16 * (n // 2 + 1))
            fn(gt[:, n % 2, :, :], gt[:, n % 2, :, :], ACT.Sigmoid).then_inc(act_sig, 1)
            if n >= 1:
                m_high(n - 1)
            if n in (2, 4):
                mix_high(1, n // 2 - 1)
        m_high(15)

        for t in range(NT):
            act.wait_ge(dve_h1, t + 1)
            act.dma_start(h1_d[t], hbs[t % 3][:, :]).then_inc(h1_saved[t % 3], 16)
            act.wait_ge(pe_h1T, t + 1)
            b0 = 4 + 2 * (t % 2)
            if t == NT - 1:
                act.wait_ge(h1_saved[2], 32)
            copy(h1T_hi[:, t, :, :],
                 ps[:, b0:b0 + 2, :].rearrange("p b (k n) -> p (b k) n", n=P)).then_inc(act_h1hi, 1)

        def u_high(b, u):
            H, f = divmod(u, FT)
            act.wait_ge(dve_us, 8 * b + u + 1)
            copy(u_hi[:, f, HALF * H:HALF * (H + 1)], us[:, u % 2, :]).then_inc(act_uhi, 1)

        def ff_block(b, first):
            for u in range(2 * FT):
                act.wait_ge(pe_up, 8 * b + u + 1)
                if not (first and u < 2):
                    act.wait_ge(dve_us, 8 * b + u - 1)
                elif u == 0:
                    h1_all_saved(act)
                    act.wait_ge(dve_h1, NT)
                fn(ur[:, u % 2, :], ps[:, u % 4, :], ACT.Relu).then_inc(act_ur, 1)
                if u >= 1:
                    u_high(b, u - 1)
            u_high(b, 2 * FT - 1)

        ff_block(0, True)
        with act.Fori(1, NBLK) as i:
            ff_block(i, False)

    @block.vector
    def _(dve):
        seq = Tally(dve_seq)
        V = nc.vector

        def mark(ins):
            ins.then_inc(dve_seq, 1)
            seq.n += 1

        def settle():
            dve.wait_ge(dve_seq, seq.now())

        def link(ins):
            mark(ins)
            settle()

        def norm(t_, mean, r, g, b):
            link(V.scalar_tensor_tensor(t_, t_, mean, g, ALU.subtract, ALU.mult))
            return V.scalar_tensor_tensor(t_, t_, r, b, ALU.mult, ALU.add)

        def row_stats(t, tile, rows=P):
            mark(V.bn_stats(stats[0:rows, t % 2, 0, :], tile[:, 0:HALF]))
            link(V.bn_stats(stats[0:rows, t % 2, 1, :], tile[:, HALF:D]))
            return V.bn_aggr(mv[0:rows, t % 2, :], stats[0:rows, t % 2, :, :].rearrange("p a b -> p (a b)"))

        def stats_x(t):
            rows = P if t < NT else META
            dve.wait_ge(x_in[t % 3], 16 * (t // 3 + 1))
            row_stats(t, xb[0:rows, t % 3, :], rows).then_inc(dve_stats, 1)

        def norm_x(t):
            rows = P if t < NT else META
            dve.wait_ge(pool_rstd, t + 1)
            tile = xb[0:rows, t % 3, :]
            norm(tile, mv[0:rows, t % 2, 0:1], rstd[0:rows, t % 2, 0:1], lng[0:rows, :], lnb[0:rows, :]
                 ).then_inc(dve_h, 1)

        def hT_low(t):
            n = P if t < NT else META
            dve.wait_ge(act_hi, t + 1)
            b0 = 4 + 2 * (t % 2)
            src = ps[:, b0:b0 + 2, :].rearrange("p b (k n) -> p (b k) n", n=P)[:, :, 0:n]
            cs = slice(P * t, P * t + n)
            V.tensor_tensor(hT_lo[:, :, cs], src, hT_hi[:, :, cs].bitcast(F32), ALU.subtract).then_inc(dve_lo, 1)

        def w_low(n):
            dve.wait_ge(act_whi, n + 1)
            V.tensor_tensor(w_lo[:, n, :], w_raw[:, n, :], w_hi[:, n, :].bitcast(F32), ALU.subtract
                            ).then_inc(dve_wlo, 1)

        stats_x(0)
        V.memset(vmb[:, :], 0.0).then_inc(dve_const, 1)
        mark(V.memset(yscale[:, 0:1], ALPHA))
        mark(V.memset(yscale[:, 1:NBLK], 1.0))
        dve.wait_ge(tab_in, 48)
        for t in range(NT + 1):
            norm_x(t)
            if t == 0:
                w_low(0)
                hT_low(0)
                stats_x(1)
                w_low(1)
            else:
                if t < NT:
                    stats_x(t + 1)
                hT_low(t)
            if t == 2:
                dve.wait_ge(small_in, 64)
                link(V.tensor_tensor(lbm[:, :], lbl[:, 0, :], lbl[:, 1, :], ALU.max))
                mark(V.tensor_tensor(lbl[:, 0, :], lbl[:, 0, :], lbm[:, :], ALU.subtract))
                V.tensor_tensor(lbl[:, 1, :], lbl[:, 1, :], lbm[:, :], ALU.subtract).then_inc(dve_lb, 1)
                link(V.tensor_scalar(negsink[:, :], sinks[:, :], -1.0, None, ALU.mult))
            if t == 4:
                dve.wait_ge(act_lb, 1)
                link(V.tensor_tensor(lbm[:, :], lbe[:, 0, :], lbe[:, 1, :], ALU.add))
                link(V.reciprocal(lbm[:, :], lbm[:, :]))
                mark(V.tensor_tensor(lb[:, :], lbe[:, 0, :], lbm[:, :], ALU.mult))
                link(V.tensor_tensor(oml[:, :], lbe[:, 1, :], lbm[:, :], ALU.mult))
                mark(V.tensor_scalar(noml[:, :], oml[:, :], -1.0, None, ALU.mult))
        dve.wait_ge(dve_h, NT + 1)
        link(V.memset(scanmask[:, :], 1.0))
        link(V.memset(scanmask[:, 0:T + 1:CHUNK], 0.0))

        def rotate(t, rows, heads, nh):
            x1, x2 = heads[:, :, 0:8], heads[:, :, 8:16]
            cos = rope[0:rows, t, 0:1, :].to_broadcast([rows, nh, 8])
            sin = rope[0:rows, t, 1:2, :].to_broadcast([rows, nh, 8])
            tmp = [rtmp[0:rows, i, 0:8 * nh].rearrange("p (h d) -> p h d", d=8) for i in range(4)]
            for o, (a, b) in zip(tmp, ((x1, cos), (x2, sin), (x2, cos), (x1, sin))):
                mark(V.tensor_tensor(o, a, b, ALU.mult))
            settle()
            mark(V.tensor_tensor(x1, tmp[0], tmp[1], ALU.subtract))
            return V.tensor_tensor(x2, tmp[2], tmp[3], ALU.add)

        dve.wait_ge(rope_in, 16)
        for t in range(NT):
            dve.wait_ge(act_tm, 10 + t)
            seen(dve, dve_rope, t)
            rotate(t, P, qtm[:, t % 2, :].rearrange("p (h d) -> p h d", d=64), QH).then_inc(dve_rope, 1)
        dve.wait_ge(dve_rope, NT)
        for t in range(NT + 1):
            rows = P if t < NT else META
            dve.wait_ge(act_tm, 18 + t)
            seen(dve, dve_krope, t)
            link(rotate(t, rows, ktm[0:rows, t % 4, :, 0, :], 2))
            V.tensor_copy(ktm[0:rows, t % 4, :, 1, :], ktm[0:rows, t % 4, :, 0, :]).then_inc(dve_krope, 1)

        for hd in range(HEADS):
            o, no = oml[:, hd:hd + 1], noml[:, hd:hd + 1]
            for H in range(2):
                v = 2 * hd + H
                idx = 16 + v
                dve.wait_ge(act_cm, 3 * hd + 2 + H)
                st_free(dve, idx)
                V.tensor_scalar(st[:, idx % 6, :], fst[:, hd, HALF * H:HALF * (H + 1)], no, o, ALU.mult, ALU.add
                                ).then_inc(dve_k, 1)
            mark(V.tensor_scalar(kmeta[:, hd, :], fst[:, hd, T:TA], no, o, ALU.mult, ALU.add))
            dve.wait_ge(dve_k, 2 * hd + 2)
            settle()
            link(V.tensor_scalar(fst[:, hd, :], fst[:, hd, :], o, lb[:, hd:hd + 1], ALU.mult, ALU.add))
            V.tensor_scalar(fst[:, hd, :], fst[:, hd, :], TINY, None, ALU.max).then_inc(dve_f, 1)
        for hd in range(HEADS):
            dve.wait_ge(act_ln, hd + 1)
            V.tensor_tensor_scan(fst[:, hd, :], scanmask[:, :], fst[:, hd, :], 0.0, ALU.mult, ALU.add
                                 ).then_inc(dve_scan, 1)
        dve.wait_ge(dve_scan, HEADS)
        V.tensor_tensor(dmeta[:, :, :], fst[:, :, TA - 1:TA].to_broadcast([P, HEADS, META]), fst[:, :, T:TA],
                        ALU.subtract).then_inc(dve_meta, 1)
        def with_qk(p):
            dve.wait_ge(act_E, p + 1)
            dve.wait_ge(qkb_in, 16 * (p + 1))
            for n, h in enumerate(LEVELS):
                half = [z.rearrange("p (q h) -> p q h", h=2 * h) for z in (X[:, n, :], pin[:, 1, :], pin[:, 0, :])]
                left = [z[:, :, 0:h] for z in half]
                right = [z[:, :, h:2 * h] for z in half]
                mark(V.tensor_tensor(left[0], left[0], left[1], ALU.mult))
                mark(V.tensor_tensor(right[0], right[0], right[2], ALU.mult))
            V.tensor_tensor(X[:, KD, :], X[:, KD, :], pin[:, 1, :], ALU.mult).then_inc(dve_X, 1)
            dve.wait_ge(act_E7, p + 1)
            V.tensor_tensor(X[:, QE, :], X[:, QE, :], pin[:, 0, :], ALU.mult).then_inc(dve_Xq, 1)

        for v in range(8, 24):
            idx = 16 + v
            dve.wait_ge(act_cm, N_FU - 8 + v + 1)
            st_free(dve, idx)
            if v < 16:
                V.tensor_tensor(st[:, idx % 6, :], ps[:, v % 4, :], sg[:, v % 2, :], ALU.mult).then_inc(dve_silu, 1)
            else:
                hd = (v - 16) // 2
                V.scalar_tensor_tensor(st[:, idx % 6, :], ps[:, v % 4, :], normg[:, hd:hd + 1], sg[:, v % 2, :],
                                       ALU.mult, ALU.mult).then_inc(dve_silu, 1)
            if v == 12:
                dve.wait_ge(act_meta, 1)
                V.tensor_tensor(dmeta[:, :, :], dmeta[:, :, :], kmeta[:, :, :], ALU.mult).then_inc(dve_kdm, 1)
            if v == 21:
                with_qk(0)

        def mix_low(H, a):
            dve.wait_ge(act_mixhi, 2 * H + a + 1)
            V.tensor_tensor(mix_lo[H][:, a, :, :], mix_raw[H][:, a, :, :], mix_hi[H][:, a, :, :].bitcast(F32),
                            ALU.subtract).then_inc(dve_mixlo, 1)

        def new_state(p, c, src, dst, bank):
            for hd in range(HEADS):
                ins = V.scalar_tensor_tensor(dst[:, hd, :], src[:, hd, :], decay[:, hd, c:c + 1],
                                             ps[:, bank, P * hd:P * (hd + 1)], ALU.mult, ALU.add)
                if hd < HEADS - 1:
                    mark(ins)
            ins.then_inc(dve_S, 1)

        def pair(p, first, last):
            one = p + 1
            dve.wait_ge(pe_lv, one)
            if first:
                dve.wait_ge(mask_in, 16)
            lv = ps[:, 4:6, :].rearrange("p b (q n) -> p (b q) n", n=256)
            mark(V.tensor_tensor(prod[:, :, :], lv[:, :, 0:LVW],
                                 masks[:, 0:LVW].rearrange("p (o n) -> p o n", o=1).to_broadcast([P, HEADS, LVW]),
                                 ALU.mult))
            V.tensor_tensor(Amat[:, :, :], lv[:, :, LVW:LVW + CHUNK],
                            masks[:, LVW:].rearrange("p (o n) -> p o n", o=1).to_broadcast([P, HEADS, CHUNK]),
                            ALU.mult).then_inc(dve_prod, 1)
            dve.wait_ge(dve_prod, one)
            settle()
            for n, h in enumerate(LEVELS):
                a = Amat[:, :, :].rearrange("p d (q h) -> p d q h", h=2 * h)[:, :, :, h:2 * h]
                pr = prod[:, :, CHUNK // 2 * n:CHUNK // 2 * (n + 1)].rearrange("p d (q h) -> p d q h", h=h)
                ins = V.tensor_tensor(a, a, pr, ALU.add)
                if n < NL - 1:
                    link(ins)
            ins.then_inc(dve_A, 1)
            dve.wait_ge(pe_U, 2 * p + 1)
            dve.wait_ge(act_dec, one)
            if first:
                st_all_saved(dve, 40)
            new_state(p, 0, S0, S1, 7)
            for g in range(2):
                dve.wait_ge(pe_sc, 2 * p + g + 1)
                sc = ps[:, 2 + 2 * g:4 + 2 * g, :].rearrange("p b (q n) -> p b q n", n=256)[:, :, :, 0:META + P]
                hs = slice(4 * g, 4 * g + 4)
                if first:
                    link(V.memset(sc[0:CHUNK, :, :, META:META + CHUNK], NEG))
                link(V.tensor_reduce(rowmax[:, hs].rearrange("p (q b) -> p b q", b=2), sc, AX, ALU.max))
                V.scalar_tensor_tensor(negmax[:, hs], rowmax[:, hs], -SCALE, negsink[:, hs], ALU.mult, ALU.min
                                       ).then_inc(dve_nb, 1)
            dve.wait_ge(dve_nb, 2 * p + 2)
            V.tensor_tensor(sinkexp[:, :], sinks[:, :], negmax[:, :], ALU.add).then_inc(dve_snk, 1)
            dve.wait_ge(act_o, one)
            link(V.tensor_tensor(osq[:, :, :], o_sb[:, :, :], o_sb[:, :, :], ALU.mult))
            V.tensor_reduce(osum[:, :], osq[:, :, :], AX, ALU.add).then_inc(dve_osum, 1)
            dve.wait_ge(pe_o, one)
            dve.wait_ge(pe_U, 2 * p + 2)
            dve.wait_ge(dve_S, 2 * p + 1)
            new_state(p, 1, S1, S0, 6)
            if not last:
                with_qk(p + 1)
            dve.wait_ge(pool_orms, one)
            V.tensor_tensor(o_sb[:, :, :], o_sb[:, :, :],
                            orms[:, :].rearrange("p (h o) -> p h o", o=1).to_broadcast([P, HEADS, P]), ALU.mult
                            ).then_inc(dve_on, 1)
            dve.wait_ge(act_es, one)
            dve.wait_ge(act_prob, 2 * p + 2)
            link(V.tensor_tensor(rden[:, :], rowsum[:, :], sinkexp[:, :], ALU.add))
            link(V.reciprocal(rden[:, :], rden[:, :]))
            if last:
                mix_low(0, 0)
            dve.wait_ge(pe_PV, one)
            V.tensor_tensor(ob[:, :, :], ps[:, 6, :].rearrange("p (h d) -> p h d", d=64),
                            rden[:, :].rearrange("p (h o) -> p h o", o=1).to_broadcast([P, QH, 64]), ALU.mult
                            ).then_inc(dve_ob, 1)
            if last:
                mix_low(0, 1)
            dve.wait_ge(pe_oT, one)
            dve.wait_ge(g_in, 16 * one)
            seen(dve, oa_saved, 16 * p)
            V.tensor_tensor(oast[:, :], ps[:, 7, :], pg[:, :], ALU.mult).then_inc(dve_oa, 1)

        pair(0, True, False)
        per_pair = 1 + (NL - 1) + 3 + 2 + 1 + 3 + 2 * NL + 2
        with dve.Fori(0, NT - 2) as i:
            seq.begin(i, per_pair)
            pair(i + 1, False, False)
        seq.end(NT - 2)
        pair(NT - 1, False, True)

        for n in range(16):
            H, j = divmod(n, KT)
            if n == 0:
                dve.wait_ge(oa_saved, 16 * NT)
                dve.wait_ge(ob_saved, 16 * NT)
            dve.wait_ge(pe_mix, n + 1)
            dve.wait_ge(act_sig, n + 1)
            seen(dve, act_mhi, n)
            seen(dve, dve_mlo, n)
            mark(V.tensor_tensor(t1[:, :], ps[:, 2 * (n % 4), :], gt[:, n % 2, 0, :], ALU.mult))
            link(V.tensor_tensor(t2[:, :], ps[:, 2 * (n % 4) + 1, :], gt[:, n % 2, 1, :], ALU.mult))
            V.tensor_tensor(t1[:, :], t1[:, :], t2[:, :], ALU.add).then_inc(dve_m, 1)
            dve.wait_ge(act_mhi, n + 1)
            hs = slice(HALF * H, HALF * (H + 1))
            V.tensor_tensor(mT_lo[:, j, hs], t1[:, :], mT_hi[:, j, hs].bitcast(F32), ALU.subtract
                            ).then_inc(dve_mlo, 1)
            if n in (2, 4):
                mix_low(1, n // 2 - 1)

        for t in range(NT):
            hb = hbs[t % 3]
            dve.wait_ge(hb_in[t % 3], 16 * (t // 3 + 1))
            dve.wait_ge(pe_wo, WO_UNITS.index((t, 1)) + 1)
            if t == 0:
                dve.wait_ge(l1_in, 32)
            banks = ps[:, 2 * (t % 2):2 * (t % 2) + 2, :].rearrange("p b n -> p (b n)")
            link(V.scalar_tensor_tensor(hb[:, :], hb[:, :], ALPHA, banks, ALU.mult, ALU.add))
            row_stats(t, hb[:, :]).then_inc(dve_r, 1)
            dve.wait_ge(pool_rstd, NT + 1 + t + 1)
            dve.wait_ge(dve_r, t + 1)
            norm(hb[:, :], mv[:, t % 2, 0:1], rstd[:, t % 2, 0:1], l1g[:, :], l1b[:, :]).then_inc(dve_h1, 1)
            dve.wait_ge(act_h1hi, t + 1)
            b0 = 4 + 2 * (t % 2)
            if t == NT - 1:
                dve.wait_ge(h1_saved[1], 48)
            V.tensor_tensor(h1T_lo[:, t, :, :], ps[:, b0:b0 + 2, :].rearrange("p b (k n) -> p (b k) n", n=P),
                            h1T_hi[:, t, :, :].bitcast(F32), ALU.subtract).then_inc(dve_h1lo, 1)

        def u_low(b, u):
            H, f = divmod(u, FT)
            hs = slice(HALF * H, HALF * (H + 1))
            dve.wait_ge(act_uhi, 8 * b + u + 1)
            V.tensor_tensor(u_lo[:, f, hs], us[:, u % 2, :], u_hi[:, f, hs].bitcast(F32), ALU.subtract
                            ).then_inc(dve_ulo, 1)

        def y_out(t):
            dve.wait_ge(pool_rstd, NT + 1 + NT + t + 1)
            dve.wait_ge(dve_r, NT + t + 1)
            norm(y[:, t, :], mv[:, t % 2, 0:1], rstd[:, t % 2, 0:1], l2g[:, :], l2b[:, :]).then_inc(dve_out, 1)

        def ff_block(b, first, last):
            for u in range(2 * FT):
                dve.wait_ge(act_ur, 8 * b + u + 1)
                if not (first and u < 2):
                    dve.wait_ge(act_uhi, 8 * b + u - 1)
                    dve.wait_ge(dve_ulo, 8 * b + u - 1)
                V.scalar_tensor_tensor(us[:, u % 2, :], ps[:, u % 4, :], 0.0, ur[:, u % 2, :], ALU.max, ALU.mult
                                       ).then_inc(dve_us, 1)
                if u >= 1:
                    u_low(b, u - 1)
            u_low(b, 2 * FT - 1)
            if first:
                dve.wait_ge(y_in, 16)
            else:
                dve.wait_ge(dve_y, 16 * b)
            for t in range(NT):
                for c in range(2):
                    n = 2 * t + c
                    dve.wait_ge(pe_down, 16 * b + n + 1)
                    yy = y[:, t, HALF * c:HALF * (c + 1)]
                    V.scalar_tensor_tensor(yy, yy, yscale[:, bass.ds(b, 1)], ps[:, 4 + n % 4, :], ALU.mult, ALU.add
                                           ).then_inc(dve_y, 1)
                if last:
                    dve.wait_ge(dve_y, 16 * b + 2 * t + 2)
                    row_stats(t, y[:, t, :]).then_inc(dve_r, 1)
                    if t == 0:
                        dve.wait_ge(l2_in, 32)
                    else:
                        y_out(t - 1)
            if last:
                y_out(NT - 1)

        ff_block(0, True, False)
        with dve.Fori(1, NBLK - 1) as i:
            ff_block(i, False, False)
        ff_block(NBLK - 1, False, True)

    block_guard.__exit__(None, None, None)
    for g in names.values():
        g.__exit__(None, None, None)
    ps_guard.__exit__(None, None, None)


_INS = ["x", "meta_tokens", "ln_emb_g", "ln_emb_b", "w_in", "b_gate", "lb_logits", "a_norm_g", "sink", "w_proj_a",
        "w_proj_b", "w_o", "ln1_g", "ln1_b", "w_up", "w_down", "ln2_g", "ln2_b"]


def constants():
    ident = np.eye(P, dtype=np.float32)
    s = np.arange(P)[:, None] % CHUNK
    parts = []
    for h in LEVELS:
        t = np.arange(CHUNK)[None, :]
        t = t[:, (t[0] // h) % 2 == 1]
        parts.append((s // (2 * h) == t // (2 * h)) & (s // h % 2 == 0))
    parts.append(s == np.arange(CHUNK)[None, :])
    mask = np.concatenate(parts, 1).astype(np.float32)
    half = 8
    inv = np.power(np.float32(500000.0), -np.arange(half, dtype=np.float32) / np.float32(half))
    pos = np.zeros((P, NT + 1), np.float32)
    pos[:, :NT] = META + np.arange(T).reshape(NT, P).T
    pos[:META, NT] = np.arange(META)
    ang = pos[:, :, None].astype(np.float32) * inv[None, None, :].astype(np.float32)
    rope = np.stack([np.cos(ang), np.sin(ang)], 2).astype(np.float32)
    return {"c_ident": ident, "c_mask": mask, "c_rope": rope}


def kernel(**inputs):
    import concourse.bacc as bacc
    from concourse.bass_utils import run_bass_kernel_spmd

    nc = bacc.Bacc("TRN2", target_bir_lowering=False, num_devices=1)
    arrays = {n: np.ascontiguousarray(inputs[n]) for n in _INS}
    arrays.update(constants())
    args = {n: nc.dram_tensor(f"in_{n}", a.shape, mybir.dt.from_np(a.dtype), kind="ExternalInput").ap()
            for n, a in arrays.items()}
    out = nc.dram_tensor("out_0", (1, T, D), F32, kind="ExternalOutput").ap()
    build(nc, out=out, **args)
    result = run_bass_kernel_spmd(nc, [{f"in_{n}": a for n, a in arrays.items()}], core_ids=[0])
    return result.results[0]["out_0"]
```
